# Optimizing a Trainium2 kernel written in Bass

```python
import jax, jax.numpy as jnp
from jax import lax
import numpy as np

D_MODEL = 1024
BATCH = 1
SEQ = 512
DEPTH = 1

N_META = 16
N_HEADS = 16
HEAD_DIM = 64
D_ATTN = N_HEADS * HEAD_DIM
D_CONV = D_MODEL
CONV_WIDTH = 31
D_FF = 4 * D_MODEL
Q_BLOCK = 128
RMS_EPS = 1e-6
LN_EPS = 1e-5

PART_SIZES = [D_ATTN, D_ATTN, D_ATTN, N_HEADS, 2 * D_CONV, D_MODEL, D_MODEL]
PART_OFFSETS = [int(o) for o in np.cumsum([0] + PART_SIZES)]
N_IN = PART_OFFSETS[-1]

kernel_name = "fox_conformer_parallel_gated_hybrid"

def rms_norm(x, g):
    xf = x.astype(jnp.float32)
    y = xf * lax.rsqrt(jnp.mean(xf * xf, axis=-1, keepdims=True) + RMS_EPS)
    return (y * g.astype(jnp.float32)).astype(x.dtype)

def layer_norm(x, g, b):
    xf = x.astype(jnp.float32)
    mu = jnp.mean(xf, axis=-1, keepdims=True)
    xc = xf - mu
    var = jnp.mean(xc * xc, axis=-1, keepdims=True)
    y = xc * lax.rsqrt(var + LN_EPS) * g.astype(jnp.float32) + b.astype(jnp.float32)
    return y.astype(x.dtype)

def forgetting_attention(q, k, v, fg_logit):
    T = q.shape[1]
    scale = HEAD_DIM ** -0.5
    log_f = jax.nn.log_sigmoid(fg_logit.astype(jnp.float32))
    cum = jnp.transpose(jnp.cumsum(log_f, axis=1), (0, 2, 1))
    starts = [0] + list(range(N_META, T, Q_BLOCK))
    ends = starts[1:] + [T]
    outs = []
    for q0, q1 in zip(starts, ends):
        s = jnp.einsum('bqhd,bkhd->bhqk', q[:, q0:q1], k[:, :q1]).astype(jnp.float32) * scale
        s = s + cum[:, :, q0:q1, None] - cum[:, :, None, :q1]
        causal = jnp.arange(q0, q1)[:, None] >= jnp.arange(q1)[None, :]
        s = jnp.where(causal, s, -jnp.inf)
        p = jax.nn.softmax(s, axis=-1).astype(v.dtype)
        outs.append(jnp.einsum('bhqk,bkhd->bqhd', p, v[:, :q1]))
    return jnp.concatenate(outs, axis=1)

def causal_depthwise_conv(u, w, b):
    C = u.shape[-1]
    y = lax.conv_general_dilated(
        u, w[:, None, :].astype(u.dtype), window_strides=(1,),
        padding=((CONV_WIDTH - 1, 0),), dimension_numbers=('NWC', 'WIO', 'NWC'),
        feature_group_count=C)
    return y + b.astype(u.dtype)

def setup_inputs(seed: int = 0) -> dict:
    key = jax.random.key(seed)
    ks = jax.random.split(key, 20)
    nrm = lambda k, shape, fan_in: jax.random.normal(k, shape, jnp.float32) * (fan_in ** -0.5)
    gain = lambda k, shape: 1.0 + 0.02 * jax.random.normal(k, shape, jnp.float32)
    small = lambda k, shape: 0.02 * jax.random.normal(k, shape, jnp.float32)
    return {
        "x": jax.random.normal(ks[0], (BATCH, SEQ, D_MODEL), jnp.float32),
        "meta_tokens": jax.random.normal(ks[1], (N_META, D_MODEL), jnp.float32),
        "norm_mix_gain": gain(ks[2], (DEPTH, D_MODEL)),
        "w_in": nrm(ks[3], (DEPTH, D_MODEL, N_IN), D_MODEL),
        "b_forget": jax.random.uniform(ks[4], (DEPTH, N_HEADS), jnp.float32, 1.0, 6.0),
        "w_attn_out": nrm(ks[5], (DEPTH, D_ATTN, D_MODEL), D_ATTN),
        "b_glu": small(ks[6], (DEPTH, 2 * D_CONV)),
        "conv_dw_w": nrm(ks[7], (DEPTH, CONV_WIDTH, D_CONV), CONV_WIDTH),
        "conv_dw_b": small(ks[8], (DEPTH, D_CONV)),
        "conv_ln_gain": gain(ks[9], (DEPTH, D_CONV)),
        "conv_ln_bias": small(ks[10], (DEPTH, D_CONV)),
        "w_conv_out": nrm(ks[11], (DEPTH, D_CONV, D_MODEL), D_CONV),
        "b_conv_out": small(ks[12], (DEPTH, D_MODEL)),
        "w_out": nrm(ks[13], (DEPTH, D_MODEL, D_MODEL), D_MODEL),
        "norm_mlp_gain": gain(ks[14], (DEPTH, D_MODEL)),
        "w_mlp_up": nrm(ks[15], (DEPTH, D_MODEL, D_FF), D_MODEL),
        "w_mlp_down": nrm(ks[16], (DEPTH, D_FF, D_MODEL), D_FF),
        "final_norm_gain": gain(ks[17], (D_MODEL,)),
    }

def reference(x, meta_tokens, norm_mix_gain, w_in, b_forget, w_attn_out, b_glu,
              conv_dw_w, conv_dw_b, conv_ln_gain, conv_ln_bias, w_conv_out, b_conv_out,
              w_out, norm_mlp_gain, w_mlp_up, w_mlp_down, final_norm_gain):
    B = x.shape[0]
    meta = jnp.broadcast_to(meta_tokens[None].astype(x.dtype), (B, N_META, D_MODEL))
    h_res = jnp.concatenate([meta, x], axis=1)
    T = h_res.shape[1]
    o = PART_OFFSETS
    for l in range(DEPTH):
        hn = rms_norm(h_res, norm_mix_gain[l])
        w_l = w_in[l]
        part = lambda i: hn @ w_l[:, o[i]:o[i + 1]]
        q = part(0).reshape(B, T, N_HEADS, HEAD_DIM)
        k = part(1).reshape(B, T, N_HEADS, HEAD_DIM)
        v = part(2).reshape(B, T, N_HEADS, HEAD_DIM)
        fg = part(3) + b_forget[l]
        glu_in = part(4) + b_glu[l]
        gate_attn = jax.nn.sigmoid(part(5))
        gate_conv = jax.nn.sigmoid(part(6))

        a = forgetting_attention(q, k, v, fg).reshape(B, T, D_ATTN) @ w_attn_out[l]

        u = glu_in[..., :D_CONV] * jax.nn.sigmoid(glu_in[..., D_CONV:])
        c = causal_depthwise_conv(u, conv_dw_w[l], conv_dw_b[l])
        c = jax.nn.silu(layer_norm(c, conv_ln_gain[l], conv_ln_bias[l]))
        c = c @ w_conv_out[l] + b_conv_out[l]

        h_res = h_res + (gate_attn * a + gate_conv * c) @ w_out[l]

        hn = rms_norm(h_res, norm_mlp_gain[l])
        h_res = h_res + jnp.square(jax.nn.relu(hn @ w_mlp_up[l])) @ w_mlp_down[l]
    y = rms_norm(h_res, final_norm_gain)
    return y[:, N_META:]


_drawn_inputs = setup_inputs


def setup_inputs(seed=0):
    import zlib

    import numpy as np

    out = dict(_drawn_inputs(seed))
    spreads = {}
    factors = {'norm_mix_gain': 5.721,
     'b_glu': 7.921,
     'conv_dw_b': 14.712,
     'conv_ln_gain': 27.247,
     'conv_ln_bias': 27.649,
     'b_conv_out': 19.56,
     'norm_mlp_gain': 8.851,
     'final_norm_gain': 8.203}
    for name, (base, spread) in spreads.items():
        noise = np.random.default_rng([zlib.crc32(name.encode()), seed]).standard_normal(out[name].shape)
        drawn = base * np.exp(spread * noise) if base else spread * noise
        out[name] = __import__('jax').numpy.asarray(drawn.astype(out[name].dtype))
    for name, factor in factors.items():
        out[name] = (out[name] * factor).astype(out[name].dtype)
    return out
```

```python
from contextlib import ExitStack

import concourse.bass as bass
from concourse import mybir

F32 = mybir.dt.float32
F32R = mybir.dt.float32r
ALU = mybir.AluOpType
ACT = mybir.ActivationFunctionType
AX_X = mybir.AxisListType.X

P = 128
D = 1024
KT = D // P
NT = 512
META = 16
T = NT + META
H = 16
HD = 64
PAIRS = H // 2
QT = NT // P
TAPS = 31
HALF = T // 2
FF = 4 * D
BLOCKS = FF // D
RMS_EPS = 1e-6
LN_EPS = 1e-5
MASKED = -1.0e30

O_Q, O_K, O_V, O_F = 0, D, 2 * D, 3 * D
O_GLU = O_F + H
O_GA = O_GLU + 2 * D
O_GC = O_GA + D

PAD = TAPS - 1 - META
UW = PAD + T
TAPS_EARLY = 13
TAPS_LATE = TAPS - TAPS_EARLY

RAW = 4
SPLIT = 2
N_F = 0
N_GLU = 1
N_PAIR = N_GLU + 2 * KT
N_GC = N_PAIR + 4 * PAIRS
N_AO = N_GC + KT
N_CO = N_AO + KT
N_WO = N_CO + KT
N_MLP = N_WO + KT
N_ALL = N_MLP + 2 * KT * BLOCKS

R_G1 = TAPS
R_BGV = TAPS + 1
R_BGS = TAPS + 2
R_CB = TAPS + 3
R_LG = TAPS + 4
R_LB = TAPS + 5
R_CO = TAPS + 6
R_G2 = TAPS + 7
NR = TAPS + 8


def build(nc, x, meta_tokens, norm_mix_gain, w_in, b_forget, w_attn_out, b_glu, conv_dw_w, conv_dw_b,
          conv_ln_gain, conv_ln_bias, w_conv_out, b_conv_out, w_out, norm_mlp_gain, w_mlp_up,
          w_mlp_down, final_norm_gain, out):
    ds = bass.ds
    with ExitStack() as ctx:
        def sb(name, shape, dt=F32):
            return ctx.enter_context(nc.sbuf_tensor(name, shape, dt))

        def sem(name):
            return ctx.enter_context(nc.semaphore(name))

        raw = sb("raw", [P, RAW, D])
        w_hi = sb("w_hi", [P, SPLIT, D], F32R)
        w_lo = sb("w_lo", [P, SPLIT, D], F32R)
        in_hi = sb("in_hi", [P, KT * T], F32R)
        in_lo = sb("in_lo", [P, KT * T], F32R)
        mid_hi = sb("mid_hi", [P, KT * NT], F32R)
        mid_lo = sb("mid_lo", [P, KT * NT], F32R)
        res = sb("res", [P, KT * NT])
        u = sb("u", [P, KT * UW])
        cv = sb("cv", [P, KT * NT])
        ga = sb("ga", [P, KT * NT])
        vT = sb("vT", [P, T])
        qT = sb("qT", [P, 2, NT])
        kT = sb("kT", [P, 2, T])
        v_real = sb("v_real", [P, 2, QT * P])
        v_meta = sb("v_meta", [META, 2, P])
        prob = sb("prob", [P, 2, T])
        pT = sb("pT", [P, 2, NT])
        pT_meta = sb("pT_meta", [META, 2, P])
        o_sb = sb("o_sb", [P, 2, QT * P])
        forget = sb("forget", [H, 2, 2 * T], F32R)
        nmax = sb("nmax", [P, 8])
        rsum = sb("rsum", [P, 8])
        rinv = sb("rinv", [P, 8])
        ident = sb("ident", [P, P])
        ident_r = sb("ident_r", [P, P], F32R)
        mask = sb("mask", [P, P])
        mask_r = sb("mask_r", [P, P], F32R)
        ones = sb("ones", [P, P])
        ones_r = sb("ones_r", [2, P], F32R)
        mean_w = sb("mean_w", [P, P])
        prm = sb("prm", [P, KT * NR])
        eps_rms = sb("eps_rms", [P, 1])
        eps_ln = sb("eps_ln", [P, 1])
        bf = sb("bf", [H, 1])
        ss = sb("ss", [P, QT + 1])
        sd = sb("sd", [P, QT + 1])
        rstd = sb("rstd", [P, QT + 1])
        bc = sb("bc", [P, 2, NT])
        decay_dram = nc.dram_tensor("decay_dram", (2, H * T), F32R, kind="Internal").ap()

        pj = ctx.enter_context(nc.psum_tensor("pj", [P, 2, 1024], F32))
        pS = ctx.enter_context(nc.psum_tensor("pS", [P, 1024], F32))
        pTO = ctx.enter_context(nc.psum_tensor("pTO", [P, 1024], F32))
        pT6 = pTO[:, 0:512]
        pO7 = pTO[:, 512:1024]


        x_tok = ga[:, :].rearrange("p (t d) -> p t d", d=D)
        xs_tok = cv[:, :].rearrange("p (t d) -> p t d", d=D)
        y_tok = x_tok
        decay = forget[0:2, :, :]
        dec_rows = forget[:, 0, :].rearrange("h (a t) -> h a t", a=2)
        x_meta = pT[0:META, :, :].rearrange("p a b -> p (a b)")
        xs_meta = prob[0:META, :, :].rearrange("p a b -> p (a b)")[:, 0:D]
        junk = o_sb[:, :, :].rearrange("p a b -> p (a b)")
        prow = u[0:NR, 0:D]
        gain_bc = u[:, 0:D]
        f_e, f_m, f_l = qT[0:H, :, :].rearrange("p a b -> p (a b)")[:, 0:T], kT[0:H, 0, :], vT[0:H, :]
        f_one = bc[0:H, :, :].rearrange("p a b -> p (a b)")[:, 0:T]

        def count(k, it=None, per=0):
            return k if it is None else it * per + k

        def wait(eng, signal, k, it=None, per=0):
            if it is None and k <= 0:
                return
            assert k > 0
            eng.wait_ge(signal, count(k, it, per))

        def par(row, m):
            return prm[:, ds(m * NR + row, 1)]

        def feat(buf, m):
            return buf[:, ds(m * NT, NT)]

        def feat_in(buf, m):
            return buf[:, ds(m * T, NT)]

        def conv_gate(m):
            return u[:, ds(m * UW, NT)]

        AT = 512 - HALF

        def prod(c, width=NT):
            return pj[:, c % 2, AT:AT + T] if width == T else pj[:, c % 2, 0:NT]

        def x_psum(m):
            return pS[:, 512 - META:1024] if m % 2 == 0 else pj[:, 1, 512 - META:1024]

        def scores(q):
            nk = META + P * (q + 1)
            at = (0, 512, 0, AT)[q]
            return pS[:, at:at + nk]

        def y_psum(t):
            return (pS[:, :], pTO[:, :], pj[:, 0, :], pj[:, 1, :])[t]

        s_raw = [sem(f"s_raw{i}") for i in range(RAW)]
        s_hi = sem("s_hi")
        s_lo = sem("s_lo")
        s_mm = sem("s_mm")
        s_ev = sem("s_ev")
        s_x = [sem(f"s_x{t}") for t in range(QT + 1)]
        s_par = sem("s_par")
        s_bf = sem("s_bf")
        s_const = sem("s_const")
        s_constr = sem("s_constr")
        s_one = sem("s_one")
        s_pT = sem("s_pT")
        s_prm = sem("s_prm")
        s_ss = sem("s_ss")
        s_sd = sem("s_sd")
        s_rstd = sem("s_rstd")
        s_xs = sem("s_xs")
        s_xT = sem("s_xT")
        s_inhi = sem("s_inhi")
        s_inlo = sem("s_inlo")
        s_rT = sem("s_rT")
        s_res = sem("s_res")
        s_f = sem("s_f")
        s_decw = sem("s_decw")
        s_dec = [sem("s_dec0"), sem("s_dec1")]
        s_pad = sem("s_pad")
        s_sig = sem("s_sig")
        s_u = sem("s_u")
        s_conv = sem("s_conv")
        s_S = sem("s_S")
        s_max = sem("s_max")
        s_exp = sem("s_exp")
        s_T = sem("s_T")
        s_pr = sem("s_pr")
        s_pm = sem("s_pm")
        s_rinv = sem("s_rinv")
        s_pv = sem("s_pv")
        s_o = sem("s_o")
        s_vT = sem("s_vT")
        s_v = sem("s_v")
        s_oT = sem("s_oT")
        s_ohi = sem("s_ohi")
        s_olo = sem("s_olo")
        s_mu = sem("s_mu")
        s_mus = sem("s_mus")
        s_xc = sem("s_xc")
        s_sq = sem("s_sq")
        s_var = sem("s_var")
        s_lsd = sem("s_lsd")
        s_lr = sem("s_lr")
        s_t = sem("s_t")
        s_y = sem("s_y")
        s_s = sem("s_s")
        s_chi = sem("s_chi")
        s_clo = sem("s_clo")
        s_gas = sem("s_gas")
        s_gcs = sem("s_gcs")
        s_mix = sem("s_mix")
        s_mhi = sem("s_mhi")
        s_mlo = sem("s_mlo")
        s_ghi = sem("s_ghi")
        s_glo = sem("s_glo")
        s_hsq = sem("s_hsq")
        s_hacc = sem("s_hacc")
        s_hsum = sem("s_hsum")
        s_hsd = sem("s_hsd")
        s_hr = sem("s_hr")
        s_relu = sem("s_relu")
        s_hf = sem("s_hf")
        s_fhi = sem("s_fhi")
        s_flo = sem("s_flo")
        s_acc = sem("s_acc")
        s_yT = sem("s_yT")
        s_yss = sem("s_yss")
        s_ysd = sem("s_ysd")
        s_yr = sem("s_yr")
        s_y4 = sem("s_y4")
        s_gain = sem("s_gain")
        s_out = sem("s_out")

        block = ctx.enter_context(nc.Block())

        @block.sync
        def _(sp):
            def load(src, c, it=None, per=4):
                if it is not None or c >= RAW:
                    wait(sp, s_hi, c - RAW + 1, it, per)
                    wait(sp, s_lo, c - RAW + 1, it, per)
                sp.dma_start(raw[:, c % RAW, :].rearrange("p (k n) -> p k n", n=P), src).then_inc(s_raw[c % RAW], 16)

            def columns(w, col, rows=None):
                src = w[0][:, ds(col, P)] if rows is None else w[0][rows, ds(col, P)]
                return src.rearrange("(k p) n -> p k n", p=P)

            for t in range(QT):
                sp.dma_start(x_tok[:, t, :], x[0, t * P:(t + 1) * P, :]).then_inc(s_x[t], 16)
            load(columns(w_in, O_F), N_F)
            for c in range(3):
                load(columns(w_in, O_GLU + (1 - c % 2) * D + c // 2 * P), N_GLU + c)
            load(columns(w_in, O_GLU + P), N_GLU + 3)
            with sp.Fori(0, KT // 2 - 1) as it:
                for c in range(4):
                    load(columns(w_in, it * (2 * P) + (O_GLU + (1 - c % 2) * D + (c // 2 + 2) * P)),
                         N_GLU + 4 + c, it)
            with sp.Fori(1, PAIRS + 1) as i:
                for c, o in enumerate((O_V, O_Q, O_K, O_GA)):
                    load(columns(w_in, i * P + (o - P)), N_PAIR - 4 + c, i)
            with sp.Fori(0, KT // 4) as it:
                for j in range(4):
                    load(columns(w_in, it * (4 * P) + (O_GC + j * P)), N_GC + j, it)
            for first, w in ((N_AO, w_attn_out), (N_CO, w_conv_out), (N_WO, w_out)):
                with sp.Fori(0, KT // 4) as it:
                    for j in range(4):
                        load(columns(w, it * (4 * P) + j * P), first + j, it)
            with sp.Fori(0, BLOCKS) as b:
                for j in range(KT):
                    load(columns(w_mlp_up, b * D + j * P), N_MLP + j, b, 2 * KT)
                for j in range(KT):
                    load(columns(w_mlp_down, j * P, ds(b * D, D)), N_MLP + KT + j, b, 2 * KT)
            sp.wait_ge(s_mix, KT)
            sp.dma_start(gain_bc, final_norm_gain.partition_broadcast(P)).then_inc(s_gain, 16)
            for t in range(QT):
                sp.wait_ge(s_y4, t + 1)
                sp.dma_start(out[0, t * P:(t + 1) * P, :], y_tok[:, t, :]).then_inc(s_out, 16)
            sp.wait_ge(s_out, 16 * QT)

        @block.gpsimd
        def _(pool):
            nc.gpsimd.memset(ident[:, :], 0.0).then_inc(s_const, 1)
            nc.gpsimd.memset(mask[:, :], 0.0).then_inc(s_const, 1)
            nc.gpsimd.memset(ones[:, :], 1.0).then_inc(s_const, 1)
            nc.gpsimd.memset(mean_w[:, :], 1.0 / D).then_inc(s_const, 1)
            nc.gpsimd.memset(eps_rms[:, :], RMS_EPS).then_inc(s_const, 1)
            nc.gpsimd.memset(eps_ln[:, :], LN_EPS).then_inc(s_const, 1)
            pool.wait_ge(s_const, 6)
            nc.gpsimd.affine_select(out=ident[:, :], in_=ident[:, :], compare_op=ALU.not_equal, fill=1.0,
                                    base=0, pattern=[[-1, P]], channel_multiplier=1).then_inc(s_const, 1)
            nc.gpsimd.affine_select(out=mask[:, :], in_=mask[:, :], compare_op=ALU.is_ge, fill=MASKED,
                                    base=0, pattern=[[-1, P]], channel_multiplier=1).then_inc(s_const, 1)
            pool.wait_ge(s_f, 9)
            for part in range(2):
                pool.dma_start(decay_dram[part, :].rearrange("(h t) -> h t", t=T),
                               dec_rows[:, part, :]).then_inc(s_decw, 16)
            pool.wait_ge(s_decw, 32)

            def rows(pair, slot):
                pool.dma_start(decay[:, slot, :], decay_dram[:, ds(pair * (2 * T), 2 * T)]).then_inc(s_dec[slot], 16)

            rows(0, 0)
            rows(1, 1)
            with pool.Fori(0, PAIRS // 2 - 1) as it:
                for slot in range(2):
                    pool.wait_ge(s_S, it * 16 + 8 * (slot + 1))
                    rows(it * 2 + (slot + 2), slot)

        @block.scalar
        def _(act):
            A = nc.scalar.activation

            def high(c, it=None, per=4):
                wait(act, s_raw[c % RAW], 16 * (c // RAW + 1), it, 16 * per // RAW)
                wait(act, s_mm, c - SPLIT + 1, it, per)
                A(w_hi[:, c % SPLIT, :], raw[:, c % RAW, :], ACT.Copy).then_inc(s_hi, 1)

            act.dma_start(x_meta, meta_tokens[:, :]).then_inc(s_x[QT], 16)
            for r0, rows, src in ((0, TAPS, conv_dw_w[0]), (R_G1, 1, norm_mix_gain),
                                  (R_BGV, 2, b_glu[0].rearrange("(a d) -> a d", d=D)), (R_CB, 1, conv_dw_b),
                                  (R_LG, 1, conv_ln_gain), (R_LB, 1, conv_ln_bias), (R_CO, 1, b_conv_out),
                                  (R_G2, 1, norm_mlp_gain)):
                act.dma_start(prow[r0:r0 + rows, :], src).then_inc(s_par, 16)
            act.dma_start(bf[:, :], b_forget.rearrange("a h -> h a")).then_inc(s_bf, 16)
            act.wait_ge(s_const, 8)
            A(ident_r[:, :], ident[:, :], ACT.Copy).then_inc(s_constr, 1)
            A(mask_r[:, :], mask[:, :], ACT.Copy).then_inc(s_constr, 1)
            A(ones_r[:, :], ones[0:2, :], ACT.Copy).then_inc(s_constr, 1)
            for t in range(QT):
                act.wait_ge(s_x[t], 16)
                wait(act, s_ss, t)
                A(junk[:, 0:D], x_tok[:, t, :], ACT.Square, accum_out=ss[:, t:t + 1]).then_inc(s_ss, 1)
            act.wait_ge(s_x[QT], 16)
            act.wait_ge(s_ss, QT)
            A(junk[0:META, 0:D], x_meta, ACT.Square, accum_out=ss[0:META, QT:QT + 1]).then_inc(s_ss, 1)
            act.wait_ge(s_ss, QT + 1)
            A(sd[:, 0:QT], ss[:, 0:QT], ACT.Sqrt, bias=eps_rms[:, :], scale=1.0 / D).then_inc(s_sd, 1)
            A(sd[0:META, QT:QT + 1], ss[0:META, QT:QT + 1], ACT.Sqrt, bias=eps_rms[0:META, :],
              scale=1.0 / D).then_inc(s_sd, 1)
            act.wait_ge(s_pT, 1)
            A(prm[:, :], pO7[:, 0:KT * NR], ACT.Copy).then_inc(s_prm, 1)
            act.wait_ge(s_prm, 1)
            for m in range(KT):
                act.wait_ge(s_xT, m + 1)
                A(in_hi[:, m * T:(m + 1) * T], x_psum(m), ACT.Copy, scale=par(R_G1, m)).then_inc(s_inhi, 1)
                if m in (1, 3):
                    high(m // 2)
            for m in range(KT):
                act.wait_ge(s_rT, m + 1)
                A(feat(res, m), pT6 if m % 2 == 0 else pO7, ACT.Copy).then_inc(s_res, 1)
            act.wait_ge(s_f, 2)
            A(f_e, f_e, ACT.Abs).then_inc(s_f, 1)
            act.wait_ge(s_f, 3)
            A(f_e, f_e, ACT.Exp, scale=-1.0).then_inc(s_f, 1)
            act.wait_ge(s_f, 4)
            A(f_e, f_e, ACT.Ln, bias=ones[0:H, 0:1]).then_inc(s_f, 1)
            act.wait_ge(s_f, 7)
            A(dec_rows[:, 0, :], f_m, ACT.Copy).then_inc(s_f, 1)

            with act.Fori(0, KT // 2) as it:
                for j in range(2):
                    m = it * 2 + j
                    high(N_GLU + 2 * j + 1, it)
                    act.wait_ge(s_mm, it * 4 + (N_GLU + 2 * j + 1))
                    act.wait_ge(s_u, it * 2 + (j + 1))
                    A(vT[:, :], prod(N_GLU + 2 * j, T), ACT.Sigmoid, bias=par(R_BGS, m)).then_inc(s_sig, 1)
                    high(N_GLU + 2 * j + 2, it)

            def softmax(s, k, it=None):
                U = 8 * k + s
                wait(act, s_max, U + 1, it, 16)
                wait(act, s_T, U - 1, it, 16)
                nk = META + P * (s % QT + 1)
                A(prob[:, s % 2, 0:nk], scores(s % QT), ACT.Exp, bias=nmax[:, s:s + 1],
                  accum_out=rsum[:, s:s + 1]).then_inc(s_exp, 1)

            def probs_real(s, k, it=None):
                U = 8 * k + s
                wait(act, s_T, U + 1, it, 16)
                wait(act, s_pv, U - 1, it, 16)
                nr = P * (s % QT + 1)
                A(pT[:, s % 2, 0:nr], pT6[:, 0:nr], ACT.Copy).then_inc(s_pr, 1)

            def out_high(k, it=None):
                wait(act, s_oT, k + 1, it, 2)
                A(feat(mid_hi, count(k, it, 2)), pT6, ACT.Copy).then_inc(s_ohi, 1)

            def pair_step(s, k, it=None):
                c = N_PAIR + 4 * k + s // 2
                if s % 2 == 0:
                    if c > N_PAIR:
                        wait(act, s_mm, c, it, 8)
                    if s == 0 and k > 0:
                        A(feat(ga, count(k - 1, it, 2)), prod(c - 1), ACT.Copy).then_inc(s_ev, 1)
                    if s == 2:
                        wait(act, s_vT, 2 * k, it, 4)
                        A(vT[:, :], prod(c - 1, T), ACT.Copy).then_inc(s_ev, 1)
                    if s == 4:
                        A(qT[:, k % 2, :], prod(c - 1), ACT.Copy, scale=HD ** -0.5).then_inc(s_ev, 1)
                    if s == 6:
                        A(kT[:, k % 2, :], prod(c - 1, T), ACT.Copy).then_inc(s_ev, 1)
                    high(c + 1, it, 8)
                attention_step(s, k, it)
                if s == 4:
                    wait(act, s_vT, 2 * k + 1, it, 4)
                    A(v_real[:, k % 2, :], pT6, ACT.Copy).then_inc(s_v, 1)
                if s == 5:
                    wait(act, s_vT, 2 * k + 2, it, 4)
                    A(v_meta[:, k % 2, :], pT6[0:META, 0:P], ACT.Copy).then_inc(s_v, 1)

            def attention_step(s, k, it=None):
                if 1 <= k <= PAIRS:
                    softmax(s, k - 1, it)
                if s == 0 and k >= 2:
                    probs_real(7, k - 2, it)
                if s > 0 and 1 <= k <= PAIRS:
                    probs_real(s - 1, k - 1, it)
                if s == 2 and k >= 2:
                    out_high(k - 2, it)

            for k in range(2):
                for s in range(8):
                    pair_step(s, k)
            with act.Fori(0, PAIRS // 2 - 1) as it:
                for k in (2, 3):
                    for s in range(8):
                        pair_step(s, k, it)
            for k in (PAIRS, PAIRS + 1):
                for s in range(8):
                    c = N_PAIR + 4 * k + s // 2
                    if s % 2 == 0:
                        act.wait_ge(s_mm, c)
                        if c == N_GC:
                            A(feat(ga, KT - 1), prod(c - 1), ACT.Copy).then_inc(s_ev, 1)
                        else:
                            act.wait_ge(s_conv, KT * TAPS)
                            A(conv_gate(c - 1 - N_GC), prod(c - 1), ACT.Copy).then_inc(s_ev, 1)
                        high(c + 1)
                    attention_step(s, k)
                    if k > PAIRS and s == 2:
                        act.wait_ge(s_mu, 1)
                        A(bc[:, 0, :], pS[:, 0:NT], ACT.Copy).then_inc(s_mus, 1)
                    if k > PAIRS and 3 <= s <= 6:
                        for m in (2 * s - 6, 2 * s - 5):
                            act.wait_ge(s_xc, m + 1)
                            wait(act, s_var, m - 1)
                            A(prob[:, m % 2, 0:NT], feat(cv, m), ACT.Square).then_inc(s_sq, 1)
            act.wait_ge(s_var, KT)
            A(bc[:, 1, :], pS[:, NT:2 * NT], ACT.Sqrt, bias=eps_ln[:, :]).then_inc(s_lsd, 1)
            act.wait_ge(s_mm, N_AO)
            A(conv_gate(KT - 1), prod(N_AO - 1), ACT.Copy).then_inc(s_ev, 1)
            act.wait_ge(s_ev, N_AO - N_PAIR)

            with act.Fori(0, KT // 4) as it:
                for j in range(4):
                    m = it * 4 + j
                    high(N_AO + j + 1, it)
                    A(feat(ga, m), feat(ga, m), ACT.Sigmoid).then_inc(s_gas, 1)
                    A(conv_gate(m), conv_gate(m), ACT.Sigmoid).then_inc(s_gcs, 1)
                    act.wait_ge(s_t, m + 1)
                    A(pT[:, 0, :], feat(cv, m), ACT.Identity, bias=par(R_LB, m), scale=par(R_LG, m)).then_inc(s_y, 1)
                    A(pT[:, 1, :], feat(cv, m), ACT.Sigmoid, bias=par(R_LB, m), scale=par(R_LG, m)).then_inc(s_y, 1)
                    act.wait_ge(s_s, m + 1)
                    A(feat_in(in_hi, m), feat(cv, m), ACT.Copy).then_inc(s_chi, 1)
            with act.Fori(0, KT // 4) as it:
                for j in range(4):
                    m = it * 4 + j
                    high(N_CO + j + 1, it)
                    act.wait_ge(s_mix, m + 1)
                    A(feat(mid_hi, m), feat(ga, m), ACT.Copy).then_inc(s_mhi, 1)
            with act.Fori(0, KT // 4) as it:
                for j in range(4):
                    m = it * 4 + j
                    high(N_WO + j + 1, it)
                    act.wait_ge(s_ev, it * 4 + (N_WO + j - N_PAIR + 1))
                    A(feat_in(in_hi, m), feat(res, m), ACT.Copy, scale=par(R_G2, m)).then_inc(s_ghi, 1)
                    A(feat(cv, m), feat(res, m), ACT.Square).then_inc(s_hsq, 1)

            def mlp(k, it=None):
                for j in range(KT):
                    c = N_MLP + 2 * KT * k + j
                    high(c + 1, it, 2 * KT)
                    if k == 0 and j == 0:
                        act.wait_ge(s_hsum, 1)
                        A(bc[:, 0, :], pS[:, 0:NT], ACT.Sqrt, bias=eps_rms[:, :]).then_inc(s_hsd, 1)
                    wait(act, s_relu, KT * k + j + 1, it, KT)
                    A(prob[:, j % 2, 0:NT], pT[:, j % 2, :], ACT.Square).then_inc(s_hf, 1)
                    wait(act, s_hf, KT * k + j + 1, it, KT)
                    A(feat(mid_hi, j), prob[:, j % 2, 0:NT], ACT.Copy).then_inc(s_fhi, 1)
                for j in range(KT):
                    c = N_MLP + 2 * KT * k + KT + j
                    if c + 1 < N_ALL:
                        high(c + 1, it, 2 * KT)

            mlp(0)
            with act.Fori(0, BLOCKS - 2) as it:
                mlp(1, it)
            mlp(BLOCKS - 1)
            for t in range(QT):
                act.wait_ge(s_yT, t + 1)
                wait(act, s_yss, t)
                A(junk[:, 0:D], y_psum(t), ACT.Square, accum_out=ss[:, t:t + 1]).then_inc(s_yss, 1)
                act.wait_ge(s_yss, t + 1)
                A(sd[:, t:t + 1], ss[:, t:t + 1], ACT.Sqrt, bias=eps_rms[:, :], scale=1.0 / D).then_inc(s_ysd, 1)

        @block.vector
        def _(dve):
            V = nc.vector

            def low(c, it=None, per=4):
                wait(dve, s_hi, c + 1, it, per)
                V.tensor_tensor(w_lo[:, c % SPLIT, :], raw[:, c % RAW, :], w_hi[:, c % SPLIT, :].bitcast(F32),
                                ALU.subtract).then_inc(s_lo, 1)

            V.memset(f_one, 1.0).then_inc(s_one, 1)
            dve.wait_ge(s_sd, 2)
            V.reciprocal(rstd[:, 0:QT], sd[:, 0:QT]).then_inc(s_rstd, 1)
            V.reciprocal(rstd[0:META, QT:QT + 1], sd[0:META, QT:QT + 1]).then_inc(s_rstd, 1)
            dve.wait_ge(s_rstd, 2)
            for t in range(QT):
                V.tensor_scalar(xs_tok[:, t, :], x_tok[:, t, :], rstd[:, t:t + 1], None, ALU.mult).then_inc(s_xs, 1)
            V.tensor_scalar(xs_meta, x_meta, rstd[0:META, QT:QT + 1], None, ALU.mult).then_inc(s_xs, 1)
            dve.wait_ge(s_prm, 1)
            V.memset(u[:, :].rearrange("p (m t) -> p m t", t=UW)[:, :, 0:PAD], 0.0).then_inc(s_pad, 1)
            for m in range(KT):
                dve.wait_ge(s_inhi, m + 1)
                V.scalar_tensor_tensor(out=in_lo[:, m * T:(m + 1) * T], in0=x_psum(m), scalar=par(R_G1, m),
                                       in1=in_hi[:, m * T:(m + 1) * T].bitcast(F32), op0=ALU.mult,
                                       op1=ALU.subtract).then_inc(s_inlo, 1)
                if m in (2, 5):
                    low(m // 3)
            dve.wait_ge(s_mm, N_F + 1)
            dve.wait_ge(s_bf, 16)
            V.tensor_scalar(f_e, prod(N_F, T)[0:H, :], bf[:, :], None, ALU.add).then_inc(s_f, 1)
            V.tensor_scalar(f_m, prod(N_F, T)[0:H, :], bf[:, :], 0.0, ALU.add, ALU.min).then_inc(s_f, 1)
            dve.wait_ge(s_f, 5)
            V.tensor_tensor(f_l, f_e, f_m, ALU.subtract).then_inc(s_f, 1)
            dve.wait_ge(s_f, 6)
            dve.wait_ge(s_one, 1)
            V.tensor_tensor_scan(f_m, f_one, f_l, 0.0, ALU.mult, ALU.add).then_inc(s_f, 1)
            dve.wait_ge(s_f, 8)
            V.tensor_tensor(dec_rows[:, 1, :], f_m, dec_rows[:, 0, :].bitcast(F32), ALU.subtract).then_inc(s_f, 1)
            low(2)
            dve.wait_ge(s_pad, 1)
            V.memset(ss[0:1, 0:1], 0.0).then_inc(s_u, 1)

            def tap(j, m, done):
                dst = feat(cv, m)
                src = u[:, ds(m * UW + j, NT)]
                if j == 0:
                    V.tensor_scalar(dst, src, par(0, m), par(R_CB, m), ALU.mult, ALU.add).then_inc(s_conv, 1)
                else:
                    dve.wait_ge(s_conv, done)
                    V.scalar_tensor_tensor(out=dst, in0=src, scalar=par(j, m), in1=dst, op0=ALU.mult,
                                           op1=ALU.add).then_inc(s_conv, 1)

            with dve.Fori(0, KT // 2) as it:
                for jj in range(2):
                    m = it * 2 + jj
                    g = N_GLU + 2 * jj
                    low(g + 2, it)
                    dve.wait_ge(s_mm, it * 4 + (g + 2))
                    dve.wait_ge(s_sig, it * 2 + (jj + 1))
                    V.scalar_tensor_tensor(out=u[:, ds(m * UW + PAD, T)], in0=prod(g + 1, T), scalar=par(R_BGV, m),
                                           in1=vT[:, :], op0=ALU.add, op1=ALU.mult).then_inc(s_u, 1)
                    dve.wait_ge(s_u, it * 2 + (jj + 2))
                    for j in range(TAPS_EARLY):
                        if j == 4:
                            low(g + 3, it)
                        tap(j, m, it * (2 * TAPS_EARLY) + (jj * TAPS_EARLY + j))

            def row_max(s, k, it=None):
                U = 8 * k + s
                wait(dve, s_S, U + 1, it, 16)
                V.tensor_reduce(nmax[:, s:s + 1], scores(s % QT), AX_X, ALU.max, negate=True).then_inc(s_max, 1)

            def meta_probs(s, k, it=None):
                U = 8 * k + s
                wait(dve, s_exp, U + 1, it, 16)
                V.reciprocal(rinv[:, s:s + 1], rsum[:, s:s + 1]).then_inc(s_rinv, 1)
                wait(dve, s_T, U + 1, it, 16)
                wait(dve, s_pv, U - 1, it, 16)
                V.tensor_copy(pT_meta[:, s % 2, :], pO7[0:META, 0:P]).then_inc(s_pm, 1)

            def head_out(s, k, it=None):
                U = 8 * k + s
                wait(dve, s_pv, U + 1, it, 16)
                wait(dve, s_rinv, U + 1, it, 16)
                at = (s % QT) * P + (s // QT) * HD
                V.tensor_scalar(o_sb[:, k % 2, at:at + HD], pO7[:, P:P + HD], rinv[:, s:s + 1], None,
                                ALU.mult).then_inc(s_o, 1)

            LATE = [len(range(s, TAPS_LATE, 8)) for s in range(8)]

            def taps(s, k, it, first, last):
                for i in range(first, last):
                    j = TAPS_EARLY + i
                    m = count(k, it, 2)
                    tap(j, m, count(KT * TAPS_EARLY + TAPS_LATE * k + i, it, 2 * TAPS_LATE))

            def attention_step(s, k, it=None):
                if 1 <= k <= PAIRS:
                    row_max(s, k - 1, it)
                t0 = sum(LATE[:s])
                if k < PAIRS:
                    taps(s, k, it, t0, t0 + 1)
                before = (7, k - 2) if s == 0 else (s - 1, k - 1)
                has = k >= 2 if s == 0 else 1 <= k <= PAIRS
                if has:
                    meta_probs(*before, it)
                if k < PAIRS:
                    taps(s, k, it, t0 + 1, t0 + LATE[s])
                if has:
                    head_out(*before, it)
                if s == 2 and k >= 2:
                    wait(dve, s_ohi, k - 1, it, 2)
                    V.tensor_tensor(feat(mid_lo, count(k - 2, it, 2)), pT6,
                                    feat(mid_hi, count(k - 2, it, 2)).bitcast(F32), ALU.subtract).then_inc(s_olo, 1)

            def pair_step(s, k, it=None):
                c = N_PAIR + 4 * k + s // 2
                if s % 2 == 0 and c > N_PAIR:
                    low(c + 1, it, 8)
                attention_step(s, k, it)

            for k in range(2):
                for s in range(8):
                    pair_step(s, k)
            with dve.Fori(0, PAIRS // 2 - 1) as it:
                for k in (2, 3):
                    for s in range(8):
                        pair_step(s, k, it)
            for k in (PAIRS, PAIRS + 1):
                for s in range(8):
                    pair_step(s, k)
                    if k > PAIRS and s == 2:
                        dve.wait_ge(s_mus, 1)
                        for m in range(KT):
                            V.tensor_tensor(feat(cv, m), feat(cv, m), bc[:, 0, :], ALU.subtract).then_inc(s_xc, 1)
            dve.wait_ge(s_lsd, 1)
            V.reciprocal(bc[:, 1, :], bc[:, 1, :]).then_inc(s_lr, 1)
            dve.wait_ge(s_lr, 1)

            with dve.Fori(0, KT // 4) as it:
                for j in range(4):
                    m = it * 4 + j
                    c = N_AO + j
                    low(c + 1, it)
                    dve.wait_ge(s_sq, KT)
                    dve.wait_ge(s_xc, KT)
                    V.tensor_tensor(feat(cv, m), feat(cv, m), bc[:, 1, :], ALU.mult).then_inc(s_t, 1)
                    dve.wait_ge(s_y, it * 8 + (2 * j + 2))
                    V.tensor_tensor(feat(cv, m), pT[:, 0, :], pT[:, 1, :], ALU.mult).then_inc(s_s, 1)
                    dve.wait_ge(s_chi, m + 1)
                    V.tensor_tensor(feat_in(in_lo, m), feat(cv, m), feat_in(in_hi, m).bitcast(F32),
                                    ALU.subtract).then_inc(s_clo, 1)
                    dve.wait_ge(s_mm, it * 4 + (c + 1))
                    dve.wait_ge(s_gas, m + 1)
                    V.tensor_tensor(feat(ga, m), prod(c), feat(ga, m), ALU.mult).then_inc(s_ev, 1)
            with dve.Fori(0, KT // 4) as it:
                for j in range(4):
                    m = it * 4 + j
                    c = N_CO + j
                    low(c + 1, it)
                    dve.wait_ge(s_mm, it * 4 + (c + 1))
                    dve.wait_ge(s_gcs, m + 1)
                    V.scalar_tensor_tensor(out=pT[:, j % 2, :], in0=prod(c), scalar=par(R_CO, m), in1=conv_gate(m),
                                           op0=ALU.add, op1=ALU.mult).then_inc(s_ev, 1)
                    dve.wait_ge(s_ev, it * 4 + (c - N_PAIR + 1))
                    V.tensor_tensor(feat(ga, m), pT[:, j % 2, :], feat(ga, m), ALU.add).then_inc(s_mix, 1)
                    dve.wait_ge(s_mhi, m + 1)
                    V.tensor_tensor(feat(mid_lo, m), feat(ga, m), feat(mid_hi, m).bitcast(F32),
                                    ALU.subtract).then_inc(s_mlo, 1)
            V.memset(bc[:, 1, :], 0.0).then_inc(s_hacc, 1)
            with dve.Fori(0, KT // 4) as it:
                for j in range(4):
                    m = it * 4 + j
                    c = N_WO + j
                    low(c + 1, it)
                    dve.wait_ge(s_mm, it * 4 + (c + 1))
                    V.tensor_tensor(feat(res, m), prod(c), feat(res, m), ALU.add).then_inc(s_ev, 1)
                    dve.wait_ge(s_ghi, m + 1)
                    V.scalar_tensor_tensor(out=feat_in(in_lo, m), in0=feat(res, m), scalar=par(R_G2, m),
                                           in1=feat_in(in_hi, m).bitcast(F32), op0=ALU.mult,
                                           op1=ALU.subtract).then_inc(s_glo, 1)
                    dve.wait_ge(s_hsq, m + 1)
                    dve.wait_ge(s_hacc, m + 1)
                    V.tensor_tensor(bc[:, 1, :], bc[:, 1, :], feat(cv, m), ALU.add).then_inc(s_hacc, 1)

            def mlp(k, it=None):
                for j in range(KT):
                    c = N_MLP + 2 * KT * k + j
                    low(c + 1, it, 2 * KT)
                    if k == 0 and j == 0:
                        dve.wait_ge(s_hsd, 1)
                        V.reciprocal(bc[:, 0, :], bc[:, 0, :]).then_inc(s_hr, 1)
                        dve.wait_ge(s_hr, 1)
                    wait(dve, s_mm, c + 1, it, 2 * KT)
                    V.scalar_tensor_tensor(out=pT[:, j % 2, :], in0=prod(c), scalar=0.0, in1=bc[:, 0, :],
                                           op0=ALU.max, op1=ALU.mult).then_inc(s_relu, 1)
                    wait(dve, s_fhi, KT * k + j + 1, it, KT)
                    V.tensor_tensor(feat(mid_lo, j), prob[:, j % 2, 0:NT], feat(mid_hi, j).bitcast(F32),
                                    ALU.subtract).then_inc(s_flo, 1)
                for j in range(KT):
                    c = N_MLP + 2 * KT * k + KT + j
                    if c + 1 < N_ALL:
                        low(c + 1, it, 2 * KT)
                    wait(dve, s_mm, c + 1, it, 2 * KT)
                    V.tensor_tensor(feat(res, j), prod(c), feat(res, j), ALU.add).then_inc(s_acc, 1)

            mlp(0)
            with dve.Fori(0, BLOCKS - 2) as it:
                mlp(1, it)
            mlp(BLOCKS - 1)
            dve.wait_ge(s_gain, 16)
            for t in range(QT):
                dve.wait_ge(s_ysd, t + 1)
                V.reciprocal(rstd[:, t:t + 1], sd[:, t:t + 1]).then_inc(s_yr, 1)
                dve.wait_ge(s_yr, t + 1)
                V.scalar_tensor_tensor(out=y_tok[:, t, :], in0=y_psum(t), scalar=rstd[:, t:t + 1], in1=gain_bc,
                                       op0=ALU.mult, op1=ALU.mult).then_inc(s_y4, 1)

        @block.tensor
        def _(pe):
            mm = nc.tensor.matmul

            def chunk(c, part, parts, rhs_hi, rhs_lo, width=NT, first=None):
                stride = T if rhs_hi is in_hi else NT
                full = width == T
                base = META if rhs_hi is in_hi and not full and c < N_AO else 0
                total = 3 * KT
                for i in range(total * part // parts, total * (part + 1) // parts):
                    kt, what = divmod(i, 3)
                    if first is not None and what == 0:
                        first(kt)
                    wt = (w_hi, w_hi, w_lo)[what][:, c % SPLIT, kt * P:(kt + 1) * P]
                    src = (rhs_hi, rhs_lo, rhs_hi)[what]
                    flags = dict(start=i == 0, stop=i == total - 1)
                    if full:
                        for h in range(2):
                            last = mm(prod(c, T)[:, h * HALF:(h + 1) * HALF], wt,
                                      src[:, kt * T + h * HALF:kt * T + (h + 1) * HALF], **flags)
                    else:
                        at = kt * stride + base
                        last = mm(prod(c), wt, src[:, at:at + NT], **flags)
                if part == parts - 1:
                    last.then_inc(s_mm, 1)

            def begin(c, it=None, per=4):
                wait(pe, s_lo, c + 1, it, per)
                if c - N_PAIR >= 2:
                    wait(pe, s_ev, c - N_PAIR - 1, it, per)

            pe.wait_ge(s_const, 8)
            pe.wait_ge(s_par, 128)
            for m in range(KT):
                last = nc.tensor.transpose(pO7[:, m * NR:(m + 1) * NR], prow[:, m * P:(m + 1) * P], ident[0:NR, 0:NR])
            last.then_inc(s_pT, 1)
            pe.wait_ge(s_xs, QT + 1)
            for m in range(KT):
                wait(pe, s_inlo, m - 1)
                dst = x_psum(m)
                nc.tensor.transpose(dst[:, 0:META], xs_meta[:, m * P:(m + 1) * P], ident[0:META, 0:META])
                for t in range(QT):
                    last = nc.tensor.transpose(dst[:, META + t * P:META + (t + 1) * P],
                                               xs_tok[:, t, m * P:(m + 1) * P], ident[:, :])
                last.then_inc(s_xT, 1)
            pe.wait_ge(s_lo, 1)
            chunk(0, 0, 1, in_hi, in_lo, T, first=lambda kt: pe.wait_ge(s_inlo, kt + 1))
            pe.wait_ge(s_prm, 1)
            for m in range(KT):
                wait(pe, s_res, m - 1)
                dst = pT6 if m % 2 == 0 else pO7
                for t in range(QT):
                    last = nc.tensor.transpose(dst[:, t * P:(t + 1) * P], x_tok[:, t, m * P:(m + 1) * P], ident[:, :])
                last.then_inc(s_rT, 1)

            pe.wait_ge(s_inlo, KT)
            pe.wait_ge(s_f, 2)
            with pe.Fori(0, KT // 2) as it:
                for j in range(2):
                    g = N_GLU + 2 * j
                    pe.wait_ge(s_lo, it * 4 + (g + 1))
                    if j == 1:
                        pe.wait_ge(s_sig, it * 2 + 1)
                    else:
                        pe.wait_ge(s_u, it * 2 + 1)
                    chunk(g, 0, 1, in_hi, in_lo, T)
                    pe.wait_ge(s_lo, it * 4 + (g + 2))
                    pe.wait_ge(s_u, it * 2 + (j + 1))
                    chunk(g + 1, 0, 1, in_hi, in_lo, T)

            def unit_scores(s, k, it=None):
                U = 8 * k + s
                h, q = divmod(s, QT)
                if s == 0:
                    wait(pe, s_ev, 4 * k + 3, it, 8)
                    wait(pe, s_dec[k % 2], 16 * (k // 2 + 1), it, 16)
                wait(pe, s_exp, U if q in (0, 3) else U - 1, it, 16)
                dst = scores(q)
                nk = META + P * (q + 1)
                rows = slice(h * HD, (h + 1) * HD)
                for a, b in (((0, nk),) if q < 3 else ((0, HALF), (HALF, nk))):
                    diagonal = b == nk
                    mm(dst[:, a:b], qT[rows, k % 2, q * P:(q + 1) * P], kT[rows, k % 2, a:b], start=True, stop=False)
                    last = mm(dst[:, a:b], ones_r[:, :], decay[:, k % 2, h * T + a:h * T + b], start=False,
                              stop=not diagonal)
                    if diagonal:
                        last = mm(dst[:, nk - P:nk], ident_r[:, :], mask_r[:, :], start=False, stop=True)
                last.then_inc(s_S, 1)

            def unit_transpose(s, k, it=None):
                U = 8 * k + s
                wait(pe, s_exp, U + 1, it, 16)
                wait(pe, s_o, U, it, 16)
                wait(pe, s_pr, U, it, 16)
                nc.tensor.transpose(pO7[:, 0:P], prob[:, s % 2, 0:P], ident[:, :])
                for t in range(s % QT + 1):
                    last = nc.tensor.transpose(pT6[:, t * P:(t + 1) * P],
                                               prob[:, s % 2, META + t * P:META + (t + 1) * P], ident[:, :])
                last.then_inc(s_T, 1)

            def unit_out(s, k, it=None):
                U = 8 * k + s
                h, q = divmod(s, QT)
                wait(pe, s_pr, U + 1, it, 16)
                wait(pe, s_pm, U + 1, it, 16)
                if s == 0:
                    wait(pe, s_v, 2 * k + 2, it, 4)
                dst = pO7[:, P:P + HD]
                mm(dst, pT_meta[:, s % 2, :], v_meta[:, k % 2, h * HD:(h + 1) * HD], start=True, stop=False)
                for t in range(q + 1):
                    last = mm(dst, pT[:, s % 2, t * P:(t + 1) * P],
                              v_real[:, k % 2, t * P + h * HD:t * P + (h + 1) * HD], start=False, stop=t == q)
                last.then_inc(s_pv, 1)

            def pair_step(s, k, it=None):
                c = N_PAIR + 4 * k + s // 2
                width = T if k < PAIRS and s // 2 in (0, 2) else NT
                part = 3 * (s % 2)
                if s % 2 == 0:
                    begin(c, it, 8)
                chunk(c, part, 6, in_hi, in_lo, width)
                has = k >= 2 if s == 0 else 1 <= k <= PAIRS
                before = (7, k - 2) if s == 0 else (s - 1, k - 1)
                if 1 <= k <= PAIRS:
                    unit_scores(s, k - 1, it)
                chunk(c, part + 1, 6, in_hi, in_lo, width)
                if has:
                    if s == 3 and k >= 2:
                        wait(pe, s_olo, k - 1, it, 2)
                    if k < PAIRS and s in (5, 6):
                        wait(pe, s_v, 2 * k + s - 4, it, 4)
                    unit_transpose(*before, it)
                chunk(c, part + 2, 6, in_hi, in_lo, width)
                if has:
                    unit_out(*before, it)
                if s == 2 and k >= 2:
                    pair_out(k - 2, it)
                if k < PAIRS and s == 4:
                    wait(pe, s_ev, 4 * k + 1, it, 8)
                    if not has:
                        pe.wait_ge(s_res, KT)
                    for t in range(QT):
                        last = nc.tensor.transpose(pT6[:, t * P:(t + 1) * P], vT[:, META + t * P:META + (t + 1) * P],
                                                   ident[:, :])
                    last.then_inc(s_vT, 1)
                if k < PAIRS and s == 5:
                    wait(pe, s_v, 2 * k + 1, it, 4)
                    nc.tensor.transpose(pT6[:, 0:P], vT[:, 0:P], ident[:, :]).then_inc(s_vT, 1)

            def pair_out(k, it=None):
                wait(pe, s_o, 8 * k + 8, it, 16)
                for q in range(QT):
                    last = nc.tensor.transpose(pT6[:, q * P:(q + 1) * P], o_sb[:, k % 2, q * P:(q + 1) * P], ident[:, :])
                last.then_inc(s_oT, 1)

            pe.wait_ge(s_sig, KT)
            pe.wait_ge(s_u, KT + 1)
            pe.wait_ge(s_constr, 3)
            for k in range(2):
                for s in range(8):
                    pair_step(s, k)
            with pe.Fori(0, PAIRS // 2 - 1) as it:
                for k in (2, 3):
                    for s in range(8):
                        pair_step(s, k, it)
            for s in range(8):
                pair_step(s, PAIRS)
            for s in range(8):
                pair_step(s, PAIRS + 1)
                if s == 1:
                    pe.wait_ge(s_conv, KT * TAPS)
                    pe.wait_ge(s_exp, 8 * PAIRS)
                    for m in range(KT):
                        last = mm(pS[:, 0:NT], mean_w[:, :], cv[:, m * NT:(m + 1) * NT], start=m == 0, stop=m == KT - 1)
                    last.then_inc(s_mu, 1)
                if 3 <= s <= 6:
                    for m in (2 * s - 6, 2 * s - 5):
                        pe.wait_ge(s_sq, m + 1)
                        mm(pS[:, NT:2 * NT], mean_w[:, :], prob[:, m % 2, 0:NT], start=m == 0,
                           stop=m == KT - 1).then_inc(s_var, 1)

            for n0, hi, lo, ready in ((N_AO, mid_hi, mid_lo, s_olo), (N_CO, in_hi, in_lo, s_clo),
                                      (N_WO, mid_hi, mid_lo, s_mlo)):
                with pe.Fori(0, KT // 4) as it:
                    for j in range(4):
                        begin(n0 + j, it)
                        chunk(n0 + j, 0, 1, hi, lo,
                              first=(lambda kt: pe.wait_ge(ready, kt + 1)) if j == 0 else None)

            def mlp_begin(c, k, j, it, up):
                wait(pe, s_lo, c + 1, it, 2 * KT)
                if k == 0 and up and j < 2:
                    pe.wait_ge(s_ev, c - N_PAIR - 1)
                elif up and j < 2:
                    wait(pe, s_acc, KT * k - 1 + j, it, KT)
                elif up:
                    wait(pe, s_relu, KT * k + j - 1, it, KT)
                elif j < 2:
                    wait(pe, s_relu, KT * (k + 1) - 1 + j, it, KT)
                else:
                    wait(pe, s_acc, KT * k + j - 1, it, KT)

            def mlp(k, it=None):
                for j in range(KT):
                    c = N_MLP + 2 * KT * k + j
                    mlp_begin(c, k, j, it, True)
                    first = (lambda kt: pe.wait_ge(s_glo, kt + 1)) if k == 0 and j == 0 else None
                    chunk(c, 0, 2, in_hi, in_lo, first=first)
                    if k == 0 and j == 0:
                        pe.wait_ge(s_glo, KT)
                    chunk(c, 1, 2, in_hi, in_lo, first=first)
                    if k == 0 and j == 0:
                        pe.wait_ge(s_hacc, KT + 1)
                        mm(pS[:, 0:NT], mean_w[:, :], bc[:, 1, :], start=True, stop=True).then_inc(s_hsum, 1)
                for j in range(KT):
                    c = N_MLP + 2 * KT * k + KT + j
                    mlp_begin(c, k, j, it, False)
                    chunk(c, 0, 1, mid_hi, mid_lo,
                          first=(lambda kt: wait(pe, s_flo, KT * k + kt + 1, it, KT)) if j == 0 else None)

            mlp(0)
            with pe.Fori(0, BLOCKS - 2) as it:
                mlp(1, it)
            mlp(BLOCKS - 1)
            for t in range(QT):
                for m in range(KT):
                    pe.wait_ge(s_acc, KT * (BLOCKS - 1) + (m + 1 if t < 2 else KT))
                    last = nc.tensor.transpose(y_psum(t)[:, m * P:(m + 1) * P], res[:, m * NT + t * P:m * NT + (t + 1) * P],
                                               ident[:, :])
                last.then_inc(s_yT, 1)


_INS = ["x", "meta_tokens", "norm_mix_gain", "w_in", "b_forget", "w_attn_out", "b_glu", "conv_dw_w", "conv_dw_b",
        "conv_ln_gain", "conv_ln_bias", "w_conv_out", "b_conv_out", "w_out", "norm_mlp_gain", "w_mlp_up",
        "w_mlp_down", "final_norm_gain"]
_OUTS = [((1, NT, D), "float32")]


def kernel(**inputs):
    import numpy as _np
    import concourse.bacc as _bacc
    from concourse import mybir as _mybir
    from concourse.bass_utils import run_bass_kernel_spmd as _run

    nc = _bacc.Bacc("TRN2", target_bir_lowering=False, num_devices=1)
    arrays, args = {}, []
    for name in _INS:
        a = _np.ascontiguousarray(inputs[name])
        arrays[f"in_{name}_dram"] = a
        args.append(nc.dram_tensor(f"in_{name}_dram", a.shape, _mybir.dt.from_np(a.dtype), kind="ExternalInput").ap())
    for i, (shape, dtype) in enumerate(_OUTS):
        dt = _mybir.dt.from_np(_np.dtype(dtype))
        args.append(nc.dram_tensor(f"out_{i}_dram", shape, dt, kind="ExternalOutput").ap())
    build(nc, *args)
    r = _run(nc, [arrays], core_ids=[0])
    got = tuple(r.results[0][f"out_{i}_dram"] for i in range(len(_OUTS)))
    return got[0]
```

```python
from contextlib import ExitStack

import concourse.bass as bass
from concourse import mybir

F32 = mybir.dt.float32
F32R = mybir.dt.float32r
ALU = mybir.AluOpType
ACT = mybir.ActivationFunctionType
AX_X = mybir.AxisListType.X

P = 128
D = 1024
KT = D // P
NT = 512
META = 16
T = NT + META
H = 16
HD = 64
PAIRS = H // 2
QT = NT // P
TAPS = 31
HALF = T // 2
FF = 4 * D
BLOCKS = FF // D
RMS_EPS = 1e-6
LN_EPS = 1e-5
MASKED = -1.0e30

O_Q, O_K, O_V, O_F = 0, D, 2 * D, 3 * D
O_GLU = O_F + H
O_GA = O_GLU + 2 * D
O_GC = O_GA + D

PAD = TAPS - 1 - META
UW = PAD + T
TAPS_EARLY = 7
TAPS_LATE = TAPS - TAPS_EARLY

RAW = 4
SPLIT = 2
N_F = 0
N_GLU = 1
N_PAIR = N_GLU + 2 * KT
N_GC = N_PAIR + 4 * PAIRS
N_AO = N_GC + KT
N_CO = N_AO + KT
N_WO = N_CO + KT
N_MLP = N_WO + KT
N_ALL = N_MLP + 2 * KT * BLOCKS

R_BGV = TAPS
R_BGS = TAPS + 1
R_CB = TAPS + 2
R_LG = TAPS + 3
R_LB = TAPS + 4
R_CO = TAPS + 5
R_G2 = TAPS + 6
NR = TAPS + 7


def build(nc, x, meta_tokens, norm_mix_gain, w_in, b_forget, w_attn_out, b_glu, conv_dw_w, conv_dw_b,
          conv_ln_gain, conv_ln_bias, w_conv_out, b_conv_out, w_out, norm_mlp_gain, w_mlp_up,
          w_mlp_down, final_norm_gain, out):
    ds = bass.ds
    with ExitStack() as ctx:
        def sb(name, shape, dt=F32):
            return ctx.enter_context(nc.sbuf_tensor(name, shape, dt))

        def sem(name):
            return ctx.enter_context(nc.semaphore(name))

        raw = sb("raw", [P, RAW, D])
        w_hi = sb("w_hi", [P, SPLIT, D], F32R)
        w_lo = sb("w_lo", [P, SPLIT, D], F32R)
        in_hi = sb("in_hi", [P, KT * T], F32R)
        in_lo = sb("in_lo", [P, KT * T], F32R)
        mid_hi = sb("mid_hi", [P, KT * NT], F32R)
        mid_lo = sb("mid_lo", [P, KT * NT], F32R)
        u = sb("u", [P, KT * UW])
        cv = sb("cv", [P, KT * NT])
        ga = sb("ga", [P, KT * NT])
        vT = sb("vT", [P, T])
        v_real = sb("v_real", [P, 2, QT * P])
        v_meta = sb("v_meta", [META, 2, P])
        prob = sb("prob", [P, 2, T])
        pT = sb("pT", [P, 2, NT])
        pT_meta = sb("pT_meta", [META, 2, P])
        o_sb = sb("o_sb", [P, 2, QT * P])
        nmax = sb("nmax", [P, 8])
        rsum = sb("rsum", [P, 8])
        rinv = sb("rinv", [P, 8])
        ident = sb("ident", [P, P])
        ident_r = sb("ident_r", [P, P], F32R)
        mask = sb("mask", [P, P])
        mask_r = sb("mask_r", [P, P], F32R)
        ones = sb("ones", [P, P])
        mean_w = sb("mean_w", [P, P])
        prm = sb("prm", [P, KT * NR])
        eps_rms = sb("eps_rms", [P, 1])
        eps_ln = sb("eps_ln", [P, 1])
        bf = sb("bf", [H, 1])
        ss = sb("ss", [P, QT + 1])
        sd = sb("sd", [P, QT + 1])
        rstd = sb("rstd", [P, QT + 1])
        with ExitStack() as pairs_only:
            k_a, k_b, q_a, q_b = (pairs_only.enter_context(nc.sbuf_tensor(name, [P, 2, 2, width], F32R))
                                  for name, width in (("k_a", T), ("k_b", T), ("q_a", NT), ("q_b", NT)))
        res = sb("res", [P, KT * NT])
        bc = sb("bc", [P, 2, NT])
        sb("rest", [P, 2 * 2 * 2 * (T + NT) - KT * NT - 2 * NT])
        decay_dram = nc.dram_tensor("decay_dram", (2, H * T), F32R, kind="Internal").ap()

        pj = ctx.enter_context(nc.psum_tensor("pj", [P, 2, 1024], F32))
        pS = ctx.enter_context(nc.psum_tensor("pS", [P, 1024], F32))
        pTO = ctx.enter_context(nc.psum_tensor("pTO", [P, 1024], F32))
        pT6 = pTO[:, 0:512]
        pO7 = pTO[:, 512:1024]


        x_tok = ga[:, :].rearrange("p (t d) -> p t d", d=D)
        xs_tok = cv[:, :].rearrange("p (t d) -> p t d", d=D)
        y_tok = x_tok
        x_again = xs_tok
        x_meta = pT[0:META, :, :].rearrange("p a b -> p (a b)")
        xs_meta = v_real[0:META, :, :].rearrange("p a b -> p (a b)")
        junk = o_sb[:, :, :].rearrange("p a b -> p (a b)")
        prow = u[0:NR, 0:D]
        gain_in = u[:, D:2 * D]
        gain_bc = u[:, 0:D]
        f_e = pT[0:H, :, :].rearrange("p a b -> p (a b)")[:, 0:T]
        f_m = o_sb[0:H, :, :].rearrange("p a b -> p (a b)")[:, 0:T]
        f_l = v_real[0:H, :, :].rearrange("p a b -> p (a b)")[:, 0:T]
        f_one = bc[0:H, :, :].rearrange("p a b -> p (a b)")[:, 0:T]
        dec_rows = prob[0:H, :, :].bitcast(F32R)

        def count(k, it=None, per=0):
            return k if it is None else it * per + k

        def wait(eng, signal, k, it=None, per=0):
            if it is None and k <= 0:
                return
            assert k > 0
            eng.wait_ge(signal, count(k, it, per))

        def par(row, m):
            return prm[:, ds(m * NR + row, 1)]

        def feat(buf, m):
            return buf[:, ds(m * NT, NT)]

        def feat_in(buf, m):
            return buf[:, ds(m * T, NT)]

        def conv_gate(m):
            return u[:, ds(m * UW, NT)]

        AT = 512 - HALF

        def prod(c, width=NT):
            return pj[:, c % 2, AT:AT + T] if width == T else pj[:, c % 2, 0:NT]

        def y_psum(t):
            return (pS[:, :], pTO[:, :], pj[:, 0, :], pj[:, 1, :])[t]

        def in_cols(buf, t):
            view = buf[:, :].rearrange("p (m t) -> p m t", t=T)
            return view[:, :, 0:META] if t == QT else view[:, :, META + t * P:META + (t + 1) * P]

        def in_psum(t):
            if t == QT:
                return pS[:, 0:KT * META].rearrange("p (m t) -> p m t", t=META)
            return y_psum(t).rearrange("p (m t) -> p m t", t=P)

        def scores(q):
            nk = META + P * (q + 1)
            at = (0, 512, 0, AT)[q]
            return pS[:, at:at + nk]

        s_raw = [sem(f"s_raw{i}") for i in range(RAW)]
        s_hi = sem("s_hi")
        s_lo = sem("s_lo")
        s_mm = sem("s_mm")
        s_ev = sem("s_ev")
        s_vev = sem("s_vev")
        s_gev = sem("s_gev")
        s_qh = sem("s_qh")
        s_kh = sem("s_kh")
        s_dup = sem("s_dup")
        s_ql = sem("s_ql")
        s_kl = sem("s_kl")
        s_one2 = sem("s_one2")
        s_g1 = sem("s_g1")
        s_again = sem("s_again")
        s_x = [sem(f"s_x{t}") for t in range(QT + 1)]
        s_par = sem("s_par")
        s_bf = sem("s_bf")
        s_const = sem("s_const")
        s_constr = sem("s_constr")
        s_one = sem("s_one")
        s_pT = sem("s_pT")
        s_ss = sem("s_ss")
        s_sd = sem("s_sd")
        s_rstd = sem("s_rstd")
        s_xs = sem("s_xs")
        s_xT = sem("s_xT")
        s_inhi = sem("s_inhi")
        s_inlo = sem("s_inlo")
        s_rT = sem("s_rT")
        s_res = sem("s_res")
        s_f = sem("s_f")
        s_decw = sem("s_decw")
        s_dec = [sem("s_dec0"), sem("s_dec1")]
        s_pad = sem("s_pad")
        s_sig = sem("s_sig")
        s_u = sem("s_u")
        s_conv = sem("s_conv")
        s_S = sem("s_S")
        s_max = sem("s_max")
        s_exp = sem("s_exp")
        s_T = sem("s_T")
        s_pr = sem("s_pr")
        s_pm = sem("s_pm")
        s_rinv = sem("s_rinv")
        s_pv = sem("s_pv")
        s_o = sem("s_o")
        s_vT = sem("s_vT")
        s_v = sem("s_v")
        s_oT = sem("s_oT")
        s_ohi = sem("s_ohi")
        s_olo = sem("s_olo")
        s_mu = sem("s_mu")
        s_mus = sem("s_mus")
        s_xc = sem("s_xc")
        s_sq = sem("s_sq")
        s_var = sem("s_var")
        s_lsd = sem("s_lsd")
        s_lr = sem("s_lr")
        s_t = sem("s_t")
        s_y = sem("s_y")
        s_s = sem("s_s")
        s_chi = sem("s_chi")
        s_clo = sem("s_clo")
        s_gas = sem("s_gas")
        s_gcs = sem("s_gcs")
        s_mix = sem("s_mix")
        s_mhi = sem("s_mhi")
        s_mlo = sem("s_mlo")
        s_ghi = sem("s_ghi")
        s_glo = sem("s_glo")
        s_hsq = sem("s_hsq")
        s_hacc = sem("s_hacc")
        s_hsum = sem("s_hsum")
        s_hsd = sem("s_hsd")
        s_hr = sem("s_hr")
        s_relu = sem("s_relu")
        s_hf = sem("s_hf")
        s_fhi = sem("s_fhi")
        s_flo = sem("s_flo")
        s_acc = sem("s_acc")
        s_yT = sem("s_yT")
        s_yss = sem("s_yss")
        s_ysd = sem("s_ysd")
        s_yr = sem("s_yr")
        s_y4 = sem("s_y4")
        s_gain = sem("s_gain")
        s_out = sem("s_out")

        block = ctx.enter_context(nc.Block())

        @block.sync
        def _(sp):
            def load(src, c, it=None, per=4):
                if it is not None or c >= RAW:
                    wait(sp, s_hi, c - RAW + 1, it, per)
                    wait(sp, s_lo, c - RAW + 1, it, per)
                sp.dma_start(raw[:, c % RAW, :].rearrange("p (k n) -> p k n", n=P), src).then_inc(s_raw[c % RAW], 16)

            def columns(w, col, rows=None):
                src = w[0][:, ds(col, P)] if rows is None else w[0][rows, ds(col, P)]
                return src.rearrange("(k p) n -> p k n", p=P)

            for t in range(QT):
                sp.dma_start(x_tok[:, t, :], x[0, t * P:(t + 1) * P, :]).then_inc(s_x[t], 16)
            load(columns(w_in, O_F), N_F)
            for c in range(3):
                load(columns(w_in, O_GLU + (1 - c % 2) * D + c // 2 * P), N_GLU + c)
            load(columns(w_in, O_GLU + P), N_GLU + 3)
            with sp.Fori(0, KT // 2 - 1) as it:
                for c in range(4):
                    load(columns(w_in, it * (2 * P) + (O_GLU + (1 - c % 2) * D + (c // 2 + 2) * P)),
                         N_GLU + 4 + c, it)
            with sp.Fori(1, PAIRS + 1) as i:
                for c, o in enumerate((O_V, O_Q, O_K, O_GA)):
                    load(columns(w_in, i * P + (o - P)), N_PAIR - 4 + c, i)
            with sp.Fori(0, KT // 4) as it:
                for j in range(4):
                    load(columns(w_in, it * (4 * P) + (O_GC + j * P)), N_GC + j, it)
            for first, w in ((N_AO, w_attn_out), (N_CO, w_conv_out), (N_WO, w_out)):
                if w is w_out:
                    sp.wait_ge(s_clo, KT)
                    sp.dma_start(x_again, x[0].rearrange("(t p) d -> p t d", p=P)).then_inc(s_again, 16)
                with sp.Fori(0, KT // 4) as it:
                    for j in range(4):
                        load(columns(w, it * (4 * P) + j * P), first + j, it)
            with sp.Fori(0, BLOCKS) as b:
                for j in range(KT):
                    load(columns(w_mlp_up, b * D + j * P), N_MLP + j, b, 2 * KT)
                for j in range(KT):
                    load(columns(w_mlp_down, j * P, ds(b * D, D)), N_MLP + KT + j, b, 2 * KT)
            sp.wait_ge(s_mix, KT)
            sp.dma_start(gain_bc, final_norm_gain.partition_broadcast(P)).then_inc(s_gain, 16)
            for t in range(QT):
                sp.wait_ge(s_y4, t + 1)
                sp.dma_start(out[0, t * P:(t + 1) * P, :], y_tok[:, t, :]).then_inc(s_out, 16)
            sp.wait_ge(s_out, 16 * QT)

        @block.gpsimd
        def _(pool):
            nc.gpsimd.memset(ident[:, :], 0.0).then_inc(s_const, 1)
            nc.gpsimd.memset(mask[:, :], 0.0).then_inc(s_const, 1)
            nc.gpsimd.memset(ones[:, :], 1.0).then_inc(s_const, 1)
            nc.gpsimd.memset(mean_w[:, :], 1.0 / D).then_inc(s_const, 1)
            nc.gpsimd.memset(eps_rms[:, :], RMS_EPS).then_inc(s_const, 1)
            nc.gpsimd.memset(eps_ln[:, :], LN_EPS).then_inc(s_const, 1)
            pool.wait_ge(s_const, 6)
            nc.gpsimd.affine_select(out=ident[:, :], in_=ident[:, :], compare_op=ALU.not_equal, fill=1.0,
                                    base=0, pattern=[[-1, P]], channel_multiplier=1).then_inc(s_const, 1)
            nc.gpsimd.affine_select(out=mask[:, :], in_=mask[:, :], compare_op=ALU.is_ge, fill=MASKED,
                                    base=0, pattern=[[-1, P]], channel_multiplier=1).then_inc(s_const, 1)
            pool.wait_ge(s_f, 9)
            for part in range(2):
                pool.dma_start(decay_dram[part, :].rearrange("(h t) -> h t", t=T),
                               dec_rows[:, part, :]).then_inc(s_decw, 16)
            pool.wait_ge(s_decw, 32)

            def rows(pair, slot):
                pool.dma_start(k_b[HD:HD + 2, slot, :, :].rearrange("p h t -> p (h t)"),
                               decay_dram[:, ds(pair * (2 * T), 2 * T)]).then_inc(s_dec[slot], 16)

            rows(0, 0)
            rows(1, 1)
            with pool.Fori(0, PAIRS // 2 - 1) as it:
                for slot in range(2):
                    pool.wait_ge(s_S, it * 16 + 8 * (slot + 1))
                    rows(it * 2 + (slot + 2), slot)

        @block.scalar
        def _(act):
            A = nc.scalar.activation

            def high(c, it=None, per=4):
                wait(act, s_raw[c % RAW], 16 * (c // RAW + 1), it, 16 * per // RAW)
                wait(act, s_mm, c - SPLIT + 1, it, per)
                A(w_hi[:, c % SPLIT, :], raw[:, c % RAW, :], ACT.Copy).then_inc(s_hi, 1)

            act.dma_start(x_meta, meta_tokens[:, :]).then_inc(s_x[QT], 16)
            act.dma_start(gain_in, norm_mix_gain[0].partition_broadcast(P)).then_inc(s_g1, 16)
            for r0, rows, src in ((0, TAPS, conv_dw_w[0]), (R_BGV, 2, b_glu[0].rearrange("(a d) -> a d", d=D)),
                                  (R_CB, 1, conv_dw_b), (R_LG, 1, conv_ln_gain), (R_LB, 1, conv_ln_bias),
                                  (R_CO, 1, b_conv_out), (R_G2, 1, norm_mlp_gain)):
                act.dma_start(prow[r0:r0 + rows, :], src).then_inc(s_par, 16)
            act.dma_start(bf[:, :], b_forget.rearrange("a h -> h a")).then_inc(s_bf, 16)
            act.wait_ge(s_const, 6)

            def token_root(i, t):
                n = P if t < QT else META
                src = x_tok[:, t, :] if t < QT else x_meta
                act.wait_ge(s_x[t], 16)
                wait(act, s_ss, i)
                A(junk[0:n, 0:D], src, ACT.Square, accum_out=ss[0:n, t:t + 1]).then_inc(s_ss, 1)
                act.wait_ge(s_ss, i + 1)
                A(sd[0:n, t:t + 1], ss[0:n, t:t + 1], ACT.Sqrt, bias=eps_rms[0:n, :], scale=1.0 / D).then_inc(s_sd, 1)

            def in_high(i, t):
                act.wait_ge(s_xT, i + 1)
                A(in_cols(in_hi, t), in_psum(t), ACT.Copy).then_inc(s_inhi, 1)

            token_root(0, QT)
            for i in range(QT):
                token_root(i + 1, i)
                if i >= 2:
                    in_high(i - 2, i - 2)
            high(0)
            in_high(2, 2)
            in_high(3, QT)
            in_high(4, 3)
            high(1)
            act.wait_ge(s_const, 8)
            A(ident_r[:, :], ident[:, :], ACT.Copy).then_inc(s_constr, 1)
            A(mask_r[:, :], mask[:, :], ACT.Copy).then_inc(s_constr, 1)
            act.wait_ge(s_pT, 1)
            A(prm[:, :], pS[:, 512:512 + KT * NR], ACT.Copy).then_inc(s_sig, 1)
            act.wait_ge(s_sig, 1)
            act.wait_ge(s_f, 2)
            A(f_e, f_e, ACT.Abs).then_inc(s_f, 1)
            act.wait_ge(s_f, 3)
            A(f_e, f_e, ACT.Exp, scale=-1.0).then_inc(s_f, 1)
            act.wait_ge(s_f, 4)
            A(f_e, f_e, ACT.Ln, bias=ones[0:H, 0:1]).then_inc(s_f, 1)

            with act.Fori(0, KT // 2) as it:
                for j in range(2):
                    m = it * 2 + j
                    high(N_GLU + 2 * j + 1, it)
                    act.wait_ge(s_mm, it * 4 + (N_GLU + 2 * j + 1))
                    act.wait_ge(s_u, it * 2 + (j + 1))
                    A(vT[:, :], prod(N_GLU + 2 * j, T), ACT.Sigmoid, bias=par(R_BGS, m)).then_inc(s_sig, 1)
                    high(N_GLU + 2 * j + 2, it)
            act.wait_ge(s_f, 7)
            A(dec_rows[:, 0, :], f_m, ACT.Copy).then_inc(s_f, 1)

            def softmax(s, k, it=None):
                U = 8 * k + s
                wait(act, s_max, U + 1, it, 16)
                wait(act, s_T, U - 1, it, 16)
                nk = META + P * (s % QT + 1)
                A(prob[:, s % 2, 0:nk], scores(s % QT), ACT.Exp, bias=nmax[:, s:s + 1],
                  accum_out=rsum[:, s:s + 1]).then_inc(s_exp, 1)

            def probs_real(s, k, it=None):
                U = 8 * k + s
                wait(act, s_T, U + 1, it, 16)
                wait(act, s_pv, U - 1, it, 16)
                nr = P * (s % QT + 1)
                A(pT_meta[:, s % 2, :], pO7[0:META, 0:P], ACT.Copy).then_inc(s_pm, 1)
                A(pT[:, s % 2, 0:nr], pT6[:, 0:nr], ACT.Copy).then_inc(s_pr, 1)

            def out_high(k, it=None):
                wait(act, s_oT, k + 1, it, 2)
                A(feat(mid_hi, count(k, it, 2)), pT6, ACT.Copy).then_inc(s_ohi, 1)

            def pair_step(s, k, it=None):
                c = N_PAIR + 4 * k + s // 2
                if s % 2 == 0 and c > N_PAIR:
                    wait(act, s_mm, c, it, 8)
                if s == 0 and k > 0:
                    A(feat(ga, count(k - 1, it, 2)), prod(c - 1), ACT.Copy).then_inc(s_gev, 1)
                if s == 2:
                    wait(act, s_vT, 2 * k, it, 4)
                    A(vT[:, :], prod(c - 1, T), ACT.Copy).then_inc(s_vev, 1)
                if s in (4, 6):
                    dst, width, scale, done = (q_a, NT, HD ** -0.5, s_qh) if s == 4 else (k_a, T, 1.0, s_kh)
                    for h in range(2):
                        A(dst[0:HD, k % 2, h, :], prod(c - 1, width)[h * HD:(h + 1) * HD, :], ACT.Copy,
                          scale=scale).then_inc(done, 1)
                attention_step(s, k, it)
                if s == 4:
                    wait(act, s_qh, 2 * k + 2, it, 4)
                    A(q_b[0:HD, k % 2, :, :], q_a[0:HD, k % 2, :, :].bitcast(F32), ACT.Copy).then_inc(s_dup, 1)
                if s == 6:
                    wait(act, s_kh, 2 * k + 2, it, 4)
                    A(k_a[HD:P, k % 2, :, :], k_a[0:HD, k % 2, :, :].bitcast(F32), ACT.Copy).then_inc(s_dup, 1)
                if s % 2 == 0:
                    high(c + 1, it, 8)
                if s == 4:
                    wait(act, s_vT, 2 * k + 1, it, 4)
                    A(v_real[:, k % 2, :], pT6, ACT.Copy).then_inc(s_v, 1)
                if s == 5:
                    wait(act, s_vT, 2 * k + 2, it, 4)
                    A(v_meta[:, k % 2, :], pT6[0:META, 0:P], ACT.Copy).then_inc(s_v, 1)

            def attention_step(s, k, it=None):
                if s == 0 and k >= 2:
                    probs_real(7, k - 2, it)
                if s > 0 and 1 <= k <= PAIRS:
                    probs_real(s - 1, k - 1, it)
                if 1 <= k <= PAIRS:
                    softmax(s, k - 1, it)
                if s == 2 and k >= 2:
                    out_high(k - 2, it)

            for k in range(2):
                for s in range(8):
                    pair_step(s, k)
            with act.Fori(0, PAIRS // 2 - 1) as it:
                for k in (2, 3):
                    for s in range(8):
                        pair_step(s, k, it)
            for k in (PAIRS, PAIRS + 1):
                for s in range(8):
                    c = N_PAIR + 4 * k + s // 2
                    if s % 2 == 0:
                        act.wait_ge(s_mm, c)
                        if c == N_GC:
                            A(feat(ga, KT - 1), prod(c - 1), ACT.Copy).then_inc(s_gev, 1)
                        else:
                            act.wait_ge(s_conv, KT * TAPS)
                            A(conv_gate(c - 1 - N_GC), prod(c - 1), ACT.Copy).then_inc(
                                s_gev if c < N_AO - 1 else s_ev, 1)
                    attention_step(s, k)
                    if s % 2 == 0:
                        high(c + 1)
                    if k > PAIRS and s == 2:
                        act.wait_ge(s_mu, 1)
                        A(bc[:, 0, :], pS[:, 0:NT], ACT.Copy).then_inc(s_mus, 1)
                    if k > PAIRS and 3 <= s <= 6:
                        for m in (2 * s - 6, 2 * s - 5):
                            act.wait_ge(s_xc, m + 1)
                            wait(act, s_var, m - 1)
                            A(prob[:, m % 2, 0:NT], feat(cv, m), ACT.Square).then_inc(s_sq, 1)
            act.wait_ge(s_var, KT)
            A(bc[:, 1, :], pS[:, NT:2 * NT], ACT.Sqrt, bias=eps_ln[:, :]).then_inc(s_lsd, 1)
            act.wait_ge(s_mm, N_AO)
            A(conv_gate(KT - 1), prod(N_AO - 1), ACT.Copy).then_inc(s_ev, 1)
            act.wait_ge(s_ev, 2)

            def conv_high(m):
                act.wait_ge(s_s, m + 1)
                A(feat_in(in_hi, m), feat(cv, m), ACT.Copy).then_inc(s_chi, 1)

            for m in range(KT):
                high(N_AO + m + 1)
                A(feat(ga, m), feat(ga, m), ACT.Sigmoid).then_inc(s_gas, 1)
                act.wait_ge(s_t, m + 1)
                A(pT[:, m % 2, :], feat(cv, m), ACT.Identity, bias=par(R_LB, m), scale=par(R_LG, m)).then_inc(s_y, 1)
                A(prob[:, m % 2, 0:NT], feat(cv, m), ACT.Sigmoid, bias=par(R_LB, m), scale=par(R_LG, m)).then_inc(s_y, 1)
                A(conv_gate(m), conv_gate(m), ACT.Sigmoid).then_inc(s_gcs, 1)
                if m:
                    conv_high(m - 1)
            conv_high(KT - 1)
            with act.Fori(0, KT // 4) as it:
                for j in range(4):
                    m = it * 4 + j
                    high(N_CO + j + 1, it)
                    act.wait_ge(s_mix, m + 1)
                    A(feat(mid_hi, m), feat(ga, m), ACT.Copy).then_inc(s_mhi, 1)
            for m in range(KT):
                high(N_WO + m + 1)
                act.wait_ge(s_rT, m + 1)
                A(feat(res, m), pT6 if m % 2 == 0 else pO7, ACT.Copy).then_inc(s_res, 1)
                act.wait_ge(s_ev, N_WO + m - N_AO + 3)
                A(feat_in(in_hi, m), feat(res, m), ACT.Copy, scale=par(R_G2, m)).then_inc(s_ghi, 1)
                wait(act, s_hacc, m)
                A(prob[:, m % 2, 0:NT], feat(res, m), ACT.Square).then_inc(s_hsq, 1)

            def mlp(k, it=None):
                for j in range(KT):
                    c = N_MLP + 2 * KT * k + j
                    high(c + 1, it, 2 * KT)
                    if k == 0 and j == 0:
                        act.wait_ge(s_hsum, 1)
                        A(bc[:, 0, :], pS[:, 0:NT], ACT.Sqrt, bias=eps_rms[:, :]).then_inc(s_hsd, 1)
                    wait(act, s_relu, KT * k + j + 1, it, KT)
                    A(prob[:, j % 2, 0:NT], pT[:, j % 2, :], ACT.Square).then_inc(s_hf, 1)
                    wait(act, s_hf, KT * k + j + 1, it, KT)
                    A(feat(mid_hi, j), prob[:, j % 2, 0:NT], ACT.Copy).then_inc(s_fhi, 1)
                for j in range(KT):
                    c = N_MLP + 2 * KT * k + KT + j
                    if c + 1 < N_ALL:
                        high(c + 1, it, 2 * KT)

            mlp(0)
            with act.Fori(0, BLOCKS - 2) as it:
                mlp(1, it)
            mlp(BLOCKS - 1)
            for t in range(QT):
                act.wait_ge(s_yT, t + 1)
                wait(act, s_yss, t)
                A(junk[:, 0:D], y_psum(t), ACT.Square, accum_out=ss[:, t:t + 1]).then_inc(s_yss, 1)
                act.wait_ge(s_yss, t + 1)
                A(sd[:, t:t + 1], ss[:, t:t + 1], ACT.Sqrt, bias=eps_rms[:, :], scale=1.0 / D).then_inc(s_ysd, 1)

        @block.vector
        def _(dve):
            V = nc.vector

            def low(c, it=None, per=4):
                wait(dve, s_hi, c + 1, it, per)
                V.tensor_tensor(w_lo[:, c % SPLIT, :], raw[:, c % RAW, :], w_hi[:, c % SPLIT, :].bitcast(F32),
                                ALU.subtract).then_inc(s_lo, 1)

            V.memset(f_one, 1.0).then_inc(s_one, 1)
            V.memset(q_b[HD:HD + 2, :, :, :].bitcast(F32), 1.0).then_inc(s_one2, 1)
            dve.wait_ge(s_g1, 16)

            def scale_tokens(i, t):
                n = P if t < QT else META
                dve.wait_ge(s_sd, i + 1)
                V.reciprocal(rstd[0:n, t:t + 1], sd[0:n, t:t + 1]).then_inc(s_rstd, 1)
                dve.wait_ge(s_rstd, i + 1)
                V.scalar_tensor_tensor(out=xs_tok[:, t, :] if t < QT else xs_meta,
                                       in0=x_tok[:, t, :] if t < QT else x_meta, scalar=rstd[0:n, t:t + 1],
                                       in1=gain_in[0:n, :], op0=ALU.mult, op1=ALU.mult).then_inc(s_xs, 1)

            def in_low(i, t):
                dve.wait_ge(s_inhi, i + 1)
                V.tensor_tensor(in_cols(in_lo, t), in_psum(t), in_cols(in_hi, t).bitcast(F32),
                                ALU.subtract).then_inc(s_inlo, 1)

            scale_tokens(0, QT)
            for i in range(QT):
                scale_tokens(i + 1, i)
                if i >= 2:
                    in_low(i - 2, i - 2)
            low(0)
            in_low(2, 2)
            in_low(3, QT)
            in_low(4, 3)
            low(1)
            dve.wait_ge(s_sig, 1)
            dve.wait_ge(s_xs, QT + 1)
            V.memset(u[:, :].rearrange("p (m t) -> p m t", t=UW)[:, :, 0:PAD], 0.0).then_inc(s_u, 1)
            dve.wait_ge(s_mm, N_F + 1)
            dve.wait_ge(s_bf, 16)
            V.tensor_scalar(f_e, prod(N_F, T)[0:H, :], bf[:, :], None, ALU.add).then_inc(s_f, 1)
            V.tensor_scalar(f_m, prod(N_F, T)[0:H, :], bf[:, :], 0.0, ALU.add, ALU.min).then_inc(s_f, 1)
            low(2)
            dve.wait_ge(s_f, 5)
            V.tensor_tensor(f_l, f_e, f_m, ALU.subtract).then_inc(s_f, 1)
            dve.wait_ge(s_f, 6)
            dve.wait_ge(s_one, 1)
            V.tensor_tensor_scan(f_m, f_one, f_l, 0.0, ALU.mult, ALU.add).then_inc(s_f, 1)

            def tap(j, m, done):
                dst = feat(cv, m)
                src = u[:, ds(m * UW + j, NT)]
                if j == 0:
                    V.tensor_scalar(dst, src, par(0, m), par(R_CB, m), ALU.mult, ALU.add).then_inc(s_conv, 1)
                else:
                    dve.wait_ge(s_conv, done)
                    V.scalar_tensor_tensor(out=dst, in0=src, scalar=par(j, m), in1=dst, op0=ALU.mult,
                                           op1=ALU.add).then_inc(s_conv, 1)

            with dve.Fori(0, KT // 2) as it:
                for jj in range(2):
                    m = it * 2 + jj
                    g = N_GLU + 2 * jj
                    low(g + 2, it)
                    dve.wait_ge(s_mm, it * 4 + (g + 2))
                    dve.wait_ge(s_sig, it * 2 + (jj + 2))
                    V.scalar_tensor_tensor(out=u[:, ds(m * UW + PAD, T)], in0=prod(g + 1, T), scalar=par(R_BGV, m),
                                           in1=vT[:, :], op0=ALU.add, op1=ALU.mult).then_inc(s_u, 1)
                    dve.wait_ge(s_u, it * 2 + (jj + 2))
                    for j in range(TAPS_EARLY):
                        if j == 3:
                            low(g + 3, it)
                        tap(j, m, it * (2 * TAPS_EARLY) + (jj * TAPS_EARLY + j))

            dve.wait_ge(s_f, 8)
            V.tensor_tensor(dec_rows[:, 1, :], f_m, dec_rows[:, 0, :].bitcast(F32), ALU.subtract).then_inc(s_f, 1)

            def row_max(s, k, it=None):
                U = 8 * k + s
                wait(dve, s_S, U + 1, it, 16)
                V.tensor_reduce(nmax[:, s:s + 1], scores(s % QT), AX_X, ALU.max, negate=True).then_inc(s_max, 1)

            def sum_reciprocal(s, k, it=None):
                U = 8 * k + s
                wait(dve, s_exp, U + 1, it, 16)
                V.reciprocal(rinv[:, s:s + 1], rsum[:, s:s + 1]).then_inc(s_rinv, 1)

            def head_out(s, k, it=None):
                U = 8 * k + s
                wait(dve, s_pv, U + 1, it, 16)
                wait(dve, s_rinv, U + 1, it, 16)
                at = (s % QT) * P + (s // QT) * HD
                V.tensor_scalar(o_sb[:, k % 2, at:at + HD], pO7[:, P:P + HD], rinv[:, s:s + 1], None,
                                ALU.mult).then_inc(s_o, 1)

            def late(k):
                return [0, 0] + [TAPS_LATE // 6] * 6 if k == 0 else [TAPS_LATE // 8] * 8

            def taps(s, k, it, first, last):
                for i in range(first, last):
                    j = TAPS_EARLY + i
                    m = count(k, it, 2)
                    tap(j, m, count(KT * TAPS_EARLY + TAPS_LATE * k + i, it, 2 * TAPS_LATE))

            def attention_step(s, k, it=None):
                if 1 <= k <= PAIRS:
                    row_max(s, k - 1, it)
                if s in (4, 6) and k < PAIRS:
                    c = N_PAIR + 4 * k + s // 2 - 1
                    hi, dst, rows, width, scale, ready, done = (
                        (q_a, q_a, slice(HD, P), NT, HD ** -0.5, s_qh, s_ql) if s == 4 else
                        (k_a, k_b, slice(0, HD), T, 1.0, s_kh, s_kl))
                    for h in range(2):
                        wait(dve, ready, 2 * k + 2, it, 4)
                        V.scalar_tensor_tensor(out=dst[rows, k % 2, h, :], in0=prod(c, width)[h * HD:(h + 1) * HD, :],
                                               scalar=scale, in1=hi[0:HD, k % 2, h, :].bitcast(F32), op0=ALU.mult,
                                               op1=ALU.subtract).then_inc(done, 1)
                t0, n = sum(late(k)[:s]), late(k)[s]
                if s % 2 == 0 and k == 0 and s > 0:
                    low(N_PAIR + s // 2 + 1)
                if k < PAIRS:
                    taps(s, k, it, t0, t0 + min(n, 1))
                before = (7, k - 2) if s == 0 else (s - 1, k - 1)
                has = k >= 2 if s == 0 else 1 <= k <= PAIRS
                if has:
                    sum_reciprocal(*before, it)
                if k < PAIRS:
                    taps(s, k, it, t0 + min(n, 1), t0 + n)
                if has:
                    head_out(*before, it)
                if s == 2 and k >= 2:
                    wait(dve, s_ohi, k - 1, it, 2)
                    V.tensor_tensor(feat(mid_lo, count(k - 2, it, 2)), pT6,
                                    feat(mid_hi, count(k - 2, it, 2)).bitcast(F32), ALU.subtract).then_inc(s_olo, 1)

            def pair_step(s, k, it=None):
                c = N_PAIR + 4 * k + s // 2
                attention_step(s, k, it)
                if s % 2 == 0 and k > 0:
                    low(c + 1, it, 8)

            for k in range(2):
                for s in range(8):
                    pair_step(s, k)
            with dve.Fori(0, PAIRS // 2 - 1) as it:
                for k in (2, 3):
                    for s in range(8):
                        pair_step(s, k, it)
            for k in (PAIRS, PAIRS + 1):
                for s in range(8):
                    pair_step(s, k)
                    if k > PAIRS and s == 2:
                        dve.wait_ge(s_mus, 1)
                        for m in range(KT):
                            V.tensor_tensor(feat(cv, m), feat(cv, m), bc[:, 0, :], ALU.subtract).then_inc(s_xc, 1)
            dve.wait_ge(s_lsd, 1)
            V.reciprocal(bc[:, 1, :], bc[:, 1, :]).then_inc(s_lr, 1)
            dve.wait_ge(s_lr, 1)

            def silu(m):
                dve.wait_ge(s_y, 2 * m + 2)
                V.tensor_tensor(feat(cv, m), pT[:, m % 2, :], prob[:, m % 2, 0:NT], ALU.mult).then_inc(s_s, 1)
                dve.wait_ge(s_chi, m + 1)
                V.tensor_tensor(feat_in(in_lo, m), feat(cv, m), feat_in(in_hi, m).bitcast(F32),
                                ALU.subtract).then_inc(s_clo, 1)

            for m in range(KT):
                c = N_AO + m
                V.tensor_tensor(feat(cv, m), feat(cv, m), bc[:, 1, :], ALU.mult).then_inc(s_t, 1)
                low(c + 1)
                if m:
                    silu(m - 1)
                dve.wait_ge(s_mm, c + 1)
                dve.wait_ge(s_gas, m + 1)
                V.tensor_tensor(feat(ga, m), prod(c), feat(ga, m), ALU.mult).then_inc(s_ev, 1)
            silu(KT - 1)
            with dve.Fori(0, KT // 4) as it:
                for j in range(4):
                    m = it * 4 + j
                    c = N_CO + j
                    low(c + 1, it)
                    dve.wait_ge(s_mm, it * 4 + (c + 1))
                    dve.wait_ge(s_gcs, m + 1)
                    V.scalar_tensor_tensor(out=pT[:, j % 2, :], in0=prod(c), scalar=par(R_CO, m), in1=conv_gate(m),
                                           op0=ALU.add, op1=ALU.mult).then_inc(s_ev, 1)
                    dve.wait_ge(s_ev, it * 4 + (c - N_AO + 3))
                    V.tensor_tensor(feat(ga, m), pT[:, j % 2, :], feat(ga, m), ALU.add).then_inc(s_mix, 1)
                    dve.wait_ge(s_mhi, m + 1)
                    V.tensor_tensor(feat(mid_lo, m), feat(ga, m), feat(mid_hi, m).bitcast(F32),
                                    ALU.subtract).then_inc(s_mlo, 1)
            V.memset(bc[:, 1, :], 0.0).then_inc(s_hacc, 1)
            for m in range(KT):
                c = N_WO + m
                low(c + 1)
                dve.wait_ge(s_mm, c + 1)
                dve.wait_ge(s_res, m + 1)
                V.tensor_tensor(feat(res, m), prod(c), feat(res, m), ALU.add).then_inc(s_ev, 1)
                dve.wait_ge(s_ghi, m + 1)
                V.scalar_tensor_tensor(out=feat_in(in_lo, m), in0=feat(res, m), scalar=par(R_G2, m),
                                       in1=feat_in(in_hi, m).bitcast(F32), op0=ALU.mult,
                                       op1=ALU.subtract).then_inc(s_glo, 1)
                dve.wait_ge(s_hsq, m + 1)
                dve.wait_ge(s_hacc, m + 1)
                V.tensor_tensor(bc[:, 1, :], bc[:, 1, :], prob[:, m % 2, 0:NT], ALU.add).then_inc(s_hacc, 1)

            def mlp(k, it=None):
                for j in range(KT):
                    c = N_MLP + 2 * KT * k + j
                    low(c + 1, it, 2 * KT)
                    if k == 0 and j == 0:
                        dve.wait_ge(s_hsd, 1)
                        V.reciprocal(bc[:, 0, :], bc[:, 0, :]).then_inc(s_hr, 1)
                        dve.wait_ge(s_hr, 1)
                    wait(dve, s_mm, c + 1, it, 2 * KT)
                    V.scalar_tensor_tensor(out=pT[:, j % 2, :], in0=prod(c), scalar=0.0, in1=bc[:, 0, :],
                                           op0=ALU.max, op1=ALU.mult).then_inc(s_relu, 1)
                    wait(dve, s_fhi, KT * k + j + 1, it, KT)
                    V.tensor_tensor(feat(mid_lo, j), prob[:, j % 2, 0:NT], feat(mid_hi, j).bitcast(F32),
                                    ALU.subtract).then_inc(s_flo, 1)
                for j in range(KT):
                    c = N_MLP + 2 * KT * k + KT + j
                    if c + 1 < N_ALL:
                        low(c + 1, it, 2 * KT)
                    wait(dve, s_mm, c + 1, it, 2 * KT)
                    V.tensor_tensor(feat(res, j), prod(c), feat(res, j), ALU.add).then_inc(s_acc, 1)

            mlp(0)
            with dve.Fori(0, BLOCKS - 2) as it:
                mlp(1, it)
            mlp(BLOCKS - 1)
            dve.wait_ge(s_gain, 16)
            for t in range(QT):
                dve.wait_ge(s_ysd, t + 1)
                V.reciprocal(rstd[:, t:t + 1], sd[:, t:t + 1]).then_inc(s_yr, 1)
                dve.wait_ge(s_yr, t + 1)
                V.scalar_tensor_tensor(out=y_tok[:, t, :], in0=y_psum(t), scalar=rstd[:, t:t + 1], in1=gain_bc,
                                       op0=ALU.mult, op1=ALU.mult).then_inc(s_y4, 1)

        @block.tensor
        def _(pe):
            mm = nc.tensor.matmul

            def chunk(c, part, parts, rhs_hi, rhs_lo, width=NT, first=None):
                stride = T if rhs_hi is in_hi else NT
                full = width == T
                base = META if c < N_AO and not full else 0
                total = 3 * KT
                for i in range(total * part // parts, total * (part + 1) // parts):
                    kt, what = divmod(i, 3)
                    if first is not None and what == 0:
                        first(kt)
                    wt = (w_hi, w_hi, w_lo)[what][:, c % SPLIT, kt * P:(kt + 1) * P]
                    src = (rhs_hi, rhs_lo, rhs_hi)[what]
                    flags = dict(start=i == 0, stop=i == total - 1)
                    if full:
                        for h in range(2):
                            last = mm(prod(c, T)[:, h * HALF:(h + 1) * HALF], wt,
                                      src[:, kt * T + h * HALF:kt * T + (h + 1) * HALF], **flags)
                    else:
                        at = kt * stride + base
                        last = mm(prod(c), wt, src[:, at:at + NT], **flags)
                if part == parts - 1:
                    last.then_inc(s_mm, 1)

            def begin(c, it=None, per=4):
                wait(pe, s_lo, c + 1, it, per)
                wait(pe, s_ev, c - N_AO + 1, it, per)

            pe.wait_ge(s_const, 8)
            for i, t in enumerate((0, 1, 2, QT, 3)):
                pe.wait_ge(s_xs, t + 2 if t < QT else 1)
                if t == QT:
                    pe.wait_ge(s_inlo, 1)
                for m in range(KT):
                    src = xs_tok[:, t, m * P:(m + 1) * P] if t < QT else xs_meta[:, m * P:(m + 1) * P]
                    n = P if t < QT else META
                    last = nc.tensor.transpose(in_psum(t)[:, m, :], src, ident[0:n, 0:n])
                last.then_inc(s_xT, 1)
            pe.wait_ge(s_par, 16 * 7)
            for m in range(KT):
                last = nc.tensor.transpose(pS[:, 512 + m * NR:512 + (m + 1) * NR], prow[:, m * P:(m + 1) * P],
                                           ident[0:NR, 0:NR])
            last.then_inc(s_pT, 1)
            pe.wait_ge(s_lo, 1)
            pe.wait_ge(s_inlo, QT + 1)
            chunk(0, 0, 1, in_hi, in_lo, T)

            with pe.Fori(0, KT // 2) as it:
                for j in range(2):
                    g = N_GLU + 2 * j
                    pe.wait_ge(s_lo, it * 4 + (g + 1))
                    pe.wait_ge(s_sig, it * 2 + (j + 1))
                    chunk(g, 0, 1, in_hi, in_lo, T)
                    pe.wait_ge(s_lo, it * 4 + (g + 2))
                    pe.wait_ge(s_u, it * 2 + (j + 1))
                    pe.wait_ge(s_f, 2)
                    chunk(g + 1, 0, 1, in_hi, in_lo, T)

            def unit_scores(s, k, it=None):
                U = 8 * k + s
                h, q = divmod(s, QT)
                if s == 0:
                    wait(pe, s_dup, 2 * k + 2, it, 4)
                    wait(pe, s_ql, 2 * k + 2, it, 4)
                    wait(pe, s_kl, 2 * k + 2, it, 4)
                    wait(pe, s_dec[k % 2], 16 * (k // 2 + 1), it, 16)
                wait(pe, s_exp, U if q in (0, 3) else U - 1, it, 16)
                dst = scores(q)
                nk = META + P * (q + 1)
                rows = HD + 2
                for a, b in (((0, nk),) if q < 3 else ((0, HALF), (HALF, nk))):
                    diagonal = b == nk
                    mm(dst[:, a:b], q_a[:, k % 2, h, q * P:(q + 1) * P], k_a[:, k % 2, h, a:b], start=True, stop=False)
                    last = mm(dst[:, a:b], q_b[0:rows, k % 2, h, q * P:(q + 1) * P], k_b[0:rows, k % 2, h, a:b],
                              start=False, stop=not diagonal)
                    if diagonal:
                        last = mm(dst[:, nk - P:nk], ident_r[:, :], mask_r[:, :], start=False, stop=True)
                last.then_inc(s_S, 1)

            def unit_transpose(s, k, it=None):
                U = 8 * k + s
                wait(pe, s_exp, U + 1, it, 16)
                wait(pe, s_o, U, it, 16)
                wait(pe, s_pr, U, it, 16)
                nc.tensor.transpose(pO7[:, 0:P], prob[:, s % 2, 0:P], ident[:, :])
                for t in range(s % QT + 1):
                    last = nc.tensor.transpose(pT6[:, t * P:(t + 1) * P],
                                               prob[:, s % 2, META + t * P:META + (t + 1) * P], ident[:, :])
                last.then_inc(s_T, 1)

            def unit_out(s, k, it=None):
                U = 8 * k + s
                h, q = divmod(s, QT)
                wait(pe, s_pr, U + 1, it, 16)
                wait(pe, s_pm, U + 1, it, 16)
                if s == 0:
                    wait(pe, s_v, 2 * k + 2, it, 4)
                dst = pO7[:, P:P + HD]
                mm(dst, pT_meta[:, s % 2, :], v_meta[:, k % 2, h * HD:(h + 1) * HD], start=True, stop=False)
                for t in range(q + 1):
                    last = mm(dst, pT[:, s % 2, t * P:(t + 1) * P],
                              v_real[:, k % 2, t * P + h * HD:t * P + (h + 1) * HD], start=False, stop=t == q)
                last.then_inc(s_pv, 1)

            def pair_step(s, k, it=None):
                c = N_PAIR + 4 * k + s // 2
                width = T if k < PAIRS and s // 2 in (0, 2) else NT
                part = 3 * (s % 2)
                if s % 2 == 0:
                    wait(pe, s_lo, c + 1, it, 8)
                    if k < PAIRS:
                        signal, n, per = ((s_kl, 2 * k, 4), (s_gev, k, 2), (s_vev, k + 1, 2), (s_ql, 2 * k + 2, 4))[s // 2]
                    elif c == N_GC:
                        signal, n, per = s_kl, 2 * PAIRS, 0
                    else:
                        signal, n, per = s_gev, c - N_GC + PAIRS - 1, 0
                    wait(pe, signal, n, it, per)
                chunk(c, part, 6, in_hi, in_lo, width)
                has = k >= 2 if s == 0 else 1 <= k <= PAIRS
                before = (7, k - 2) if s == 0 else (s - 1, k - 1)
                if 1 <= k <= PAIRS:
                    unit_scores(s, k - 1, it)
                chunk(c, part + 1, 6, in_hi, in_lo, width)
                if has:
                    if s == 3 and k >= 2:
                        wait(pe, s_olo, k - 1, it, 2)
                    if k < PAIRS and s in (5, 6):
                        wait(pe, s_v, 2 * k + s - 4, it, 4)
                    unit_transpose(*before, it)
                chunk(c, part + 2, 6, in_hi, in_lo, width)
                if has:
                    unit_out(*before, it)
                if s == 2 and k >= 2:
                    pair_out(k - 2, it)
                if k < PAIRS and s == 4:
                    wait(pe, s_vev, k + 1, it, 2)
                    for t in range(QT):
                        last = nc.tensor.transpose(pT6[:, t * P:(t + 1) * P], vT[:, META + t * P:META + (t + 1) * P],
                                                   ident[:, :])
                    last.then_inc(s_vT, 1)
                if k < PAIRS and s == 5:
                    wait(pe, s_v, 2 * k + 1, it, 4)
                    nc.tensor.transpose(pT6[:, 0:P], vT[:, 0:P], ident[:, :]).then_inc(s_vT, 1)

            def pair_out(k, it=None):
                wait(pe, s_o, 8 * k + 8, it, 16)
                for q in range(QT):
                    last = nc.tensor.transpose(pT6[:, q * P:(q + 1) * P], o_sb[:, k % 2, q * P:(q + 1) * P], ident[:, :])
                last.then_inc(s_oT, 1)

            pe.wait_ge(s_sig, KT + 1)
            pe.wait_ge(s_u, KT + 1)
            pe.wait_ge(s_constr, 2)
            pe.wait_ge(s_one2, 1)
            for k in range(2):
                for s in range(8):
                    pair_step(s, k)
            with pe.Fori(0, PAIRS // 2 - 1) as it:
                for k in (2, 3):
                    for s in range(8):
                        pair_step(s, k, it)
            for s in range(8):
                pair_step(s, PAIRS)
            for s in range(8):
                pair_step(s, PAIRS + 1)
                if s == 1:
                    pe.wait_ge(s_conv, KT * TAPS)
                    pe.wait_ge(s_exp, 8 * PAIRS)
                    for m in range(KT):
                        last = mm(pS[:, 0:NT], mean_w[:, :], cv[:, m * NT:(m + 1) * NT], start=m == 0, stop=m == KT - 1)
                    last.then_inc(s_mu, 1)
                if 3 <= s <= 6:
                    for m in (2 * s - 6, 2 * s - 5):
                        pe.wait_ge(s_sq, m + 1)
                        mm(pS[:, NT:2 * NT], mean_w[:, :], prob[:, m % 2, 0:NT], start=m == 0,
                           stop=m == KT - 1).then_inc(s_var, 1)

            for n0, hi, lo, ready in ((N_AO, mid_hi, mid_lo, s_olo), (N_CO, in_hi, in_lo, s_clo)):
                with pe.Fori(0, KT // 4) as it:
                    for j in range(4):
                        begin(n0 + j, it)
                        chunk(n0 + j, 0, 1, hi, lo,
                              first=(lambda kt: pe.wait_ge(ready, kt + 1)) if j == 0 else None)

            for m in range(KT):
                c = N_WO + m
                begin(c)
                wait(pe, s_again, 16 if m == 0 else 0)
                for t in range(QT):
                    last = nc.tensor.transpose((pT6 if m % 2 == 0 else pO7)[:, t * P:(t + 1) * P],
                                               x_again[:, t, m * P:(m + 1) * P], ident[:, :])
                last.then_inc(s_rT, 1)
                chunk(c, 0, 1, mid_hi, mid_lo, first=(lambda kt: pe.wait_ge(s_mlo, kt + 1)) if m == 0 else None)

            def mlp_begin(c, k, j, it, up):
                wait(pe, s_lo, c + 1, it, 2 * KT)
                if k == 0 and up and j < 2:
                    pe.wait_ge(s_ev, c - N_AO + 1)
                elif up and j < 2:
                    wait(pe, s_acc, KT * k - 1 + j, it, KT)
                elif up:
                    wait(pe, s_relu, KT * k + j - 1, it, KT)
                elif j < 2:
                    wait(pe, s_relu, KT * (k + 1) - 1 + j, it, KT)
                else:
                    wait(pe, s_acc, KT * k + j - 1, it, KT)

            def mlp(k, it=None):
                for j in range(KT):
                    c = N_MLP + 2 * KT * k + j
                    mlp_begin(c, k, j, it, True)
                    first = (lambda kt: pe.wait_ge(s_glo, kt + 1)) if k == 0 and j == 0 else None
                    chunk(c, 0, 2, in_hi, in_lo, first=first)
                    if k == 0 and j == 0:
                        pe.wait_ge(s_hacc, KT + 1)
                        mm(pS[:, 0:NT], mean_w[:, :], bc[:, 1, :], start=True, stop=True).then_inc(s_hsum, 1)
                    chunk(c, 1, 2, in_hi, in_lo, first=first)
                for j in range(KT):
                    c = N_MLP + 2 * KT * k + KT + j
                    mlp_begin(c, k, j, it, False)
                    chunk(c, 0, 1, mid_hi, mid_lo,
                          first=(lambda kt: wait(pe, s_flo, KT * k + kt + 1, it, KT)) if j == 0 else None)

            mlp(0)
            with pe.Fori(0, BLOCKS - 2) as it:
                mlp(1, it)
            mlp(BLOCKS - 1)
            for t in range(QT):
                for m in range(KT):
                    pe.wait_ge(s_acc, KT * (BLOCKS - 1) + (m + 1 if t < 2 else KT))
                    last = nc.tensor.transpose(y_psum(t)[:, m * P:(m + 1) * P], res[:, m * NT + t * P:m * NT + (t + 1) * P],
                                               ident[:, :])
                last.then_inc(s_yT, 1)


_INS = ["x", "meta_tokens", "norm_mix_gain", "w_in", "b_forget", "w_attn_out", "b_glu", "conv_dw_w", "conv_dw_b",
        "conv_ln_gain", "conv_ln_bias", "w_conv_out", "b_conv_out", "w_out", "norm_mlp_gain", "w_mlp_up",
        "w_mlp_down", "final_norm_gain"]
_OUTS = [((1, NT, D), "float32")]


def kernel(**inputs):
    import numpy as _np
    import concourse.bacc as _bacc
    from concourse import mybir as _mybir
    from concourse.bass_utils import run_bass_kernel_spmd as _run

    nc = _bacc.Bacc("TRN2", target_bir_lowering=False, num_devices=1)
    arrays, args = {}, []
    for name in _INS:
        a = _np.ascontiguousarray(inputs[name])
        arrays[f"in_{name}_dram"] = a
        args.append(nc.dram_tensor(f"in_{name}_dram", a.shape, _mybir.dt.from_np(a.dtype), kind="ExternalInput").ap())
    for i, (shape, dtype) in enumerate(_OUTS):
        dt = _mybir.dt.from_np(_np.dtype(dtype))
        args.append(nc.dram_tensor(f"out_{i}_dram", shape, dt, kind="ExternalOutput").ap())
    build(nc, *args)
    r = _run(nc, [arrays], core_ids=[0])
    got = tuple(r.results[0][f"out_{i}_dram"] for i in range(len(_OUTS)))
    return got[0]
```

```python
from contextlib import ExitStack

import concourse.bass as bass
from concourse import mybir

F32 = mybir.dt.float32
F32R = mybir.dt.float32r
ALU = mybir.AluOpType
ACT = mybir.ActivationFunctionType
AX_X = mybir.AxisListType.X

P = 128
D = 1024
KT = D // P
NT = 512
META = 16
T = NT + META
H = 16
HD = 64
PAIRS = H // 2
QT = NT // P
TAPS = 31
HALF = T // 2
FF = 4 * D
BLOCKS = FF // D
RMS_EPS = 1e-6
LN_EPS = 1e-5
MASKED = -1.0e30

O_Q, O_K, O_V, O_F = 0, D, 2 * D, 3 * D
O_GLU = O_F + H
O_GA = O_GLU + 2 * D
O_GC = O_GA + D

PAD = TAPS - 1 - META
UW = PAD + T
TAPS_EARLY = 7
TAPS_MID = 1
TAPS_LATE = TAPS - TAPS_EARLY - TAPS_MID
TAPS_STEP = (3, 3, 3, 3, 3, 3, 2, 3)
MID_STEP = (0, 0, 2, 2, 0, 0, 2, 2)
assert sum(TAPS_STEP) == TAPS_LATE and sum(MID_STEP) == KT * TAPS_MID

SQ_POOL = 5

RAW = 4
SPLIT = 2
N_F = 0
N_GLU = 1
N_PAIR = N_GLU + 2 * KT
N_GC = N_PAIR + 4 * PAIRS
N_AO = N_GC + KT
N_CO = N_AO + KT
N_WO = N_CO + KT
N_MLP = N_WO + KT
N_ALL = N_MLP + 2 * KT * BLOCKS

R_BGV = TAPS
R_BGS = TAPS + 1
R_CB = TAPS + 2
R_LG = TAPS + 3
R_LB = TAPS + 4
R_CO = TAPS + 5
R_G2 = TAPS + 6
NR = TAPS + 7


def build(nc, x, meta_tokens, norm_mix_gain, w_in, b_forget, w_attn_out, b_glu, conv_dw_w, conv_dw_b,
          conv_ln_gain, conv_ln_bias, w_conv_out, b_conv_out, w_out, norm_mlp_gain, w_mlp_up,
          w_mlp_down, final_norm_gain, out):
    ds = bass.ds
    with ExitStack() as ctx:
        def sb(name, shape, dt=F32):
            return ctx.enter_context(nc.sbuf_tensor(name, shape, dt))

        def sem(name):
            return ctx.enter_context(nc.semaphore(name))

        raw = sb("raw", [P, RAW, D])
        w_hi = sb("w_hi", [P, SPLIT, D], F32R)
        w_lo = sb("w_lo", [P, SPLIT, D], F32R)
        in_hi = sb("in_hi", [P, KT * T], F32R)
        in_lo = sb("in_lo", [P, KT * T], F32R)
        mid_hi = sb("mid_hi", [P, KT * NT], F32R)
        mid_lo = sb("mid_lo", [P, KT * NT], F32R)
        u = sb("u", [P, KT * UW])
        cv = sb("cv", [P, KT * NT])
        ga = sb("ga", [P, KT * NT])
        vT = sb("vT", [P, T])
        v_real = sb("v_real", [P, 2, QT * P])
        v_meta = sb("v_meta", [META, 2, P])
        conv_sum = sb("conv_sum", [P, NT])
        prob = sb("prob", [P, 2, T])
        pT = sb("pT", [P, 2, NT])
        pT_meta = sb("pT_meta", [META, 2, P])
        o_sb = sb("o_sb", [P, 2, QT * P])
        nmax = sb("nmax", [P, 8])
        rsum = sb("rsum", [P, 8])
        rinv = sb("rinv", [P, 8])
        ident = sb("ident", [P, P])
        ident_r = sb("ident_r", [P, P], F32R)
        mask = sb("mask", [P, P])
        mask_r = sb("mask_r", [P, P], F32R)
        ones = sb("ones", [P, P])
        mean_w = sb("mean_w", [P, P])
        prm = sb("prm", [P, KT * NR])
        eps_rms = sb("eps_rms", [P, 1])
        eps_ln = sb("eps_ln", [P, 1])
        bf = sb("bf", [H, 1])
        ss = sb("ss", [P, QT + 1])
        sd = sb("sd", [P, QT + 1])
        rstd = sb("rstd", [P, QT + 1])
        with ExitStack() as pairs_only:
            k_a, k_b, q_a, q_b = (pairs_only.enter_context(nc.sbuf_tensor(name, [P, 2, 2, width], F32R))
                                  for name, width in (("k_a", T), ("k_b", T), ("q_a", NT), ("q_b", NT)))
        res = sb("res", [P, KT * NT])
        bc = sb("bc", [P, 2, NT])
        sb("rest", [P, 2 * 2 * 2 * (T + NT) - KT * NT - 2 * NT])
        decay_dram = nc.dram_tensor("decay_dram", (2, H * T), F32R, kind="Internal").ap()

        pj = ctx.enter_context(nc.psum_tensor("pj", [P, 2, 1024], F32))
        pS = ctx.enter_context(nc.psum_tensor("pS", [P, 1024], F32))
        pTO = ctx.enter_context(nc.psum_tensor("pTO", [P, 1024], F32))
        pT6 = pTO[:, 0:512]
        pO7 = pTO[:, 512:1024]


        x_tok = ga[:, :].rearrange("p (t d) -> p t d", d=D)
        xs_tok = cv[:, :].rearrange("p (t d) -> p t d", d=D)
        y_tok = x_tok
        x_again = xs_tok
        sq_sum = res[:, 0:NT]
        x_meta = pT[0:META, :, :].rearrange("p a b -> p (a b)")
        xs_meta = v_real[0:META, :, :].rearrange("p a b -> p (a b)")
        junk = o_sb[:, :, :].rearrange("p a b -> p (a b)")
        prow = u[0:NR, 0:D]
        gain_in = u[:, D:2 * D]
        gain_bc = u[:, 0:D]
        f_e = pT[0:H, :, :].rearrange("p a b -> p (a b)")[:, 0:T]
        f_m = o_sb[0:H, :, :].rearrange("p a b -> p (a b)")[:, 0:T]
        f_l = v_real[0:H, :, :].rearrange("p a b -> p (a b)")[:, 0:T]
        f_one = bc[0:H, :, :].rearrange("p a b -> p (a b)")[:, 0:T]
        dec_rows = prob[0:H, :, :].bitcast(F32R)

        def count(k, it=None, per=0):
            return k if it is None else it * per + k

        def wait(eng, signal, k, it=None, per=0):
            if it is None and k <= 0:
                return
            assert k > 0
            eng.wait_ge(signal, count(k, it, per))

        def par(row, m):
            return prm[:, ds(m * NR + row, 1)]

        def feat(buf, m):
            return buf[:, ds(m * NT, NT)]

        def feat_in(buf, m):
            return buf[:, ds(m * T, NT)]

        def conv_gate(m):
            return u[:, ds(m * UW, NT)]

        AT = 512 - HALF

        def prod(c, width=NT):
            return pj[:, c % 2, AT:AT + T] if width == T else pj[:, c % 2, 0:NT]

        HALVES = ((N_ALL - 2, 0), (N_ALL - 1, 0), (N_ALL - 2, 1), (N_ALL - 1, 1))
        HT = NT // 2

        def half_prod(c, h):
            return pj[:, c % 2, 512 * h:512 * h + HT]

        def y_psum(t):
            return (pS[:, :], pTO[:, :], pj[:, 1, :], pj[:, 0, :])[t]

        def in_cols(buf, t):
            view = buf[:, :].rearrange("p (m t) -> p m t", t=T)
            return view[:, :, 0:META] if t == QT else view[:, :, META + t * P:META + (t + 1) * P]

        ORDER = (QT,) + tuple(range(QT))

        def in_psum(t):
            if t == QT:
                return pj[:, 1, 0:KT * META].rearrange("p (m t) -> p m t", t=META)
            return (pS[:, :], pTO[:, :], pj[:, 1, :], pS[:, :])[t].rearrange("p (m t) -> p m t", t=P)

        def scores(q):
            nk = META + P * (q + 1)
            at = (0, 512, 0, AT)[q]
            return pS[:, at:at + nk]

        s_raw = [sem(f"s_raw{i}") for i in range(RAW)]
        s_hi = sem("s_hi")
        s_lo = sem("s_lo")
        s_mm = sem("s_mm")
        s_ev = sem("s_ev")
        s_vev = sem("s_vev")
        s_gev = sem("s_gev")
        s_qh = sem("s_qh")
        s_kh = sem("s_kh")
        s_dup = sem("s_dup")
        s_ql = sem("s_ql")
        s_kl = sem("s_kl")
        s_one2 = sem("s_one2")
        s_g1 = sem("s_g1")
        s_again = sem("s_again")
        s_x = [sem(f"s_x{t}") for t in range(QT + 1)]
        s_par = sem("s_par")
        s_bf = sem("s_bf")
        s_const = sem("s_const")
        s_constr = sem("s_constr")
        s_one = sem("s_one")
        s_pT = sem("s_pT")
        s_ss = sem("s_ss")
        s_sd = sem("s_sd")
        s_rstd = sem("s_rstd")
        s_xs = sem("s_xs")
        s_xT = sem("s_xT")
        s_inhi = sem("s_inhi")
        s_inlo = sem("s_inlo")
        s_rT = sem("s_rT")
        s_res = sem("s_res")
        s_f = sem("s_f")
        s_decw = sem("s_decw")
        s_dec = [sem("s_dec0"), sem("s_dec1")]
        s_pad = sem("s_pad")
        s_sig = sem("s_sig")
        s_u = sem("s_u")
        s_conv = sem("s_conv")
        s_S = sem("s_S")
        s_max = sem("s_max")
        s_exp = sem("s_exp")
        s_T = sem("s_T")
        s_pr = sem("s_pr")
        s_pm = sem("s_pm")
        s_rinv = sem("s_rinv")
        s_pv = sem("s_pv")
        s_o = sem("s_o")
        s_vT = sem("s_vT")
        s_v = sem("s_v")
        s_oT = sem("s_oT")
        s_ohi = sem("s_ohi")
        s_olo = sem("s_olo")
        s_csum = sem("s_csum")
        s_sqsum = sem("s_sqsum")
        s_mu = sem("s_mu")
        s_mus = sem("s_mus")
        s_xc = sem("s_xc")
        s_sq = sem("s_sq")
        s_var = sem("s_var")
        s_lsd = sem("s_lsd")
        s_lr = sem("s_lr")
        s_t = sem("s_t")
        s_y = sem("s_y")
        s_s = sem("s_s")
        s_chi = sem("s_chi")
        s_clo = sem("s_clo")
        s_gas = sem("s_gas")
        s_gcs = sem("s_gcs")
        s_mix = sem("s_mix")
        s_mhi = sem("s_mhi")
        s_mlo = sem("s_mlo")
        s_ghi = sem("s_ghi")
        s_glo = sem("s_glo")
        s_hsq = sem("s_hsq")
        s_hacc = sem("s_hacc")
        s_hsum = sem("s_hsum")
        s_hsd = sem("s_hsd")
        s_hr = sem("s_hr")
        s_relu = sem("s_relu")
        s_hf = sem("s_hf")
        s_fhi = sem("s_fhi")
        s_flo = sem("s_flo")
        s_acc = sem("s_acc")
        s_half = sem("s_half")
        s_yT = sem("s_yT")
        s_yss = sem("s_yss")
        s_ysd = sem("s_ysd")
        s_yr = sem("s_yr")
        s_y4 = sem("s_y4")
        s_gain = sem("s_gain")
        s_out = sem("s_out")

        block = ctx.enter_context(nc.Block())

        @block.sync
        def _(sp):
            def load(src, c, it=None, per=4):
                if it is not None or c >= RAW:
                    wait(sp, s_hi, c - RAW + 1, it, per)
                    wait(sp, s_lo, c - RAW + 1, it, per)
                sp.dma_start(raw[:, c % RAW, :].rearrange("p (k n) -> p k n", n=P), src).then_inc(s_raw[c % RAW], 16)

            def columns(w, col, rows=None):
                src = w[0][:, ds(col, P)] if rows is None else w[0][rows, ds(col, P)]
                return src.rearrange("(k p) n -> p k n", p=P)

            for t in range(QT):
                sp.dma_start(x_tok[:, t, :], x[0, t * P:(t + 1) * P, :]).then_inc(s_x[t], 16)
                if t == 0:
                    sp.dma_start(gain_in, norm_mix_gain[0].partition_broadcast(P)).then_inc(s_g1, 16)
                if t == 2:
                    load(columns(w_in, O_F), N_F)
            for c in range(3):
                load(columns(w_in, O_GLU + (1 - c % 2) * D + c // 2 * P), N_GLU + c)
            load(columns(w_in, O_GLU + P), N_GLU + 3)
            with sp.Fori(0, KT // 2 - 1) as it:
                for c in range(4):
                    load(columns(w_in, it * (2 * P) + (O_GLU + (1 - c % 2) * D + (c // 2 + 2) * P)),
                         N_GLU + 4 + c, it)
            with sp.Fori(1, PAIRS + 1) as i:
                for c, o in enumerate((O_V, O_Q, O_K, O_GA)):
                    load(columns(w_in, i * P + (o - P)), N_PAIR - 4 + c, i)
            with sp.Fori(0, KT // 4) as it:
                for j in range(4):
                    load(columns(w_in, it * (4 * P) + (O_GC + j * P)), N_GC + j, it)
            for first, w in ((N_AO, w_attn_out), (N_CO, w_conv_out), (N_WO, w_out)):
                if w is w_out:
                    sp.wait_ge(s_clo, KT)
                    sp.dma_start(x_again, x[0].rearrange("(t p) d -> p t d", p=P)).then_inc(s_again, 16)
                with sp.Fori(0, KT // 4) as it:
                    for j in range(4):
                        load(columns(w, it * (4 * P) + j * P), first + j, it)
            with sp.Fori(0, BLOCKS) as b:
                for j in range(KT):
                    load(columns(w_mlp_up, b * D + j * P), N_MLP + j, b, 2 * KT)
                for j in range(KT):
                    load(columns(w_mlp_down, j * P, ds(b * D, D)), N_MLP + KT + j, b, 2 * KT)
            sp.wait_ge(s_mix, KT)
            sp.dma_start(gain_bc, final_norm_gain.partition_broadcast(P)).then_inc(s_gain, 16)
            for t in range(QT):
                sp.wait_ge(s_y4, t + 1)
                sp.dma_start(out[0, t * P:(t + 1) * P, :], y_tok[:, t, :]).then_inc(s_out, 16)
            sp.wait_ge(s_out, 16 * QT)

        @block.gpsimd
        def _(pool):
            nc.gpsimd.memset(eps_rms[:, :], RMS_EPS).then_inc(s_const, 1)
            nc.gpsimd.memset(ident[:, :], 0.0).then_inc(s_const, 1)
            nc.gpsimd.memset(mask[:, :], 0.0).then_inc(s_const, 1)
            nc.gpsimd.memset(ones[:, :], 1.0).then_inc(s_const, 1)
            nc.gpsimd.memset(mean_w[:, :], 1.0 / D).then_inc(s_const, 1)
            nc.gpsimd.memset(eps_ln[:, :], LN_EPS).then_inc(s_const, 1)
            pool.wait_ge(s_const, 6)
            nc.gpsimd.affine_select(out=ident[:, :], in_=ident[:, :], compare_op=ALU.not_equal, fill=1.0,
                                    base=0, pattern=[[-1, P]], channel_multiplier=1).then_inc(s_const, 1)
            nc.gpsimd.affine_select(out=mask[:, :], in_=mask[:, :], compare_op=ALU.is_ge, fill=MASKED,
                                    base=0, pattern=[[-1, P]], channel_multiplier=1).then_inc(s_const, 1)
            for r0, rows, src in ((0, TAPS, conv_dw_w[0]), (R_BGV, 2, b_glu[0].rearrange("(a d) -> a d", d=D)),
                                  (R_CB, 1, conv_dw_b), (R_LG, 1, conv_ln_gain), (R_LB, 1, conv_ln_bias),
                                  (R_CO, 1, b_conv_out), (R_G2, 1, norm_mlp_gain)):
                pool.dma_start(prow[r0:r0 + rows, :], src).then_inc(s_par, 16)
            pool.dma_start(bf[:, :], b_forget.rearrange("a h -> h a")).then_inc(s_bf, 16)
            pool.wait_ge(s_f, 9)
            for part in range(2):
                pool.dma_start(decay_dram[part, :].rearrange("(h t) -> h t", t=T),
                               dec_rows[:, part, :]).then_inc(s_decw, 16)
            pool.wait_ge(s_decw, 32)

            def rows_back(pair, slot):
                pool.dma_start(k_b[HD:HD + 2, slot, :, :].rearrange("p h t -> p (h t)"),
                               decay_dram[:, ds(pair * (2 * T), 2 * T)]).then_inc(s_dec[slot], 16)

            rows_back(0, 0)
            rows_back(1, 1)
            nc.gpsimd.memset(conv_sum[:, :], 0.0).then_inc(s_csum, 1)

            def add_conv(m, it=None):
                wait(pool, s_conv, KT * (TAPS_EARLY + TAPS_MID) + TAPS_LATE * (m + 1), it, 2 * TAPS_LATE)
                wait(pool, s_csum, m + 1, it, 2)
                nc.gpsimd.tensor_tensor(conv_sum[:, :], conv_sum[:, :], feat(cv, count(m, it, 2)), ALU.add).then_inc(s_csum, 1)

            with pool.Fori(0, PAIRS // 2 - 1) as it:
                for slot in range(2):
                    pool.wait_ge(s_S, it * 16 + 8 * (slot + 1))
                    rows_back(it * 2 + (slot + 2), slot)
                    add_conv(slot, it)
            add_conv(KT - 2)
            add_conv(KT - 1)
            pool.wait_ge(s_S, 8 * PAIRS)
            nc.gpsimd.memset(sq_sum, 0.0).then_inc(s_sqsum, 1)
            for m in range(SQ_POOL):
                pool.wait_ge(s_sq, m + 1)
                pool.wait_ge(s_sqsum, m + 1)
                nc.gpsimd.tensor_tensor(sq_sum, sq_sum, prob[:, m % 2, 0:NT], ALU.add).then_inc(s_sqsum, 1)

        @block.scalar
        def _(act):
            A = nc.scalar.activation

            def high(c, it=None, per=4):
                wait(act, s_raw[c % RAW], 16 * (c // RAW + 1), it, 16 * per // RAW)
                wait(act, s_mm, c - SPLIT + 1, it, per)
                A(w_hi[:, c % SPLIT, :], raw[:, c % RAW, :], ACT.Copy).then_inc(s_hi, 1)

            act.dma_start(x_meta, meta_tokens[:, :]).then_inc(s_x[QT], 16)
            act.wait_ge(s_const, 1)
            A(sd[:, 0:1], eps_rms[:, :], ACT.Sqrt).then_inc(s_sd, 1)
            act.wait_ge(s_sd, 1)

            def token_root(i, t):
                n = P if t < QT else META
                src = x_tok[:, t, :] if t < QT else x_meta
                act.wait_ge(s_x[t], 16)
                wait(act, s_ss, i)
                A(junk[0:n, 0:D], src, ACT.Square, accum_out=ss[0:n, t:t + 1]).then_inc(s_ss, 1)
                act.wait_ge(s_ss, i + 1)
                A(sd[0:n, t:t + 1], ss[0:n, t:t + 1], ACT.Sqrt, bias=eps_rms[0:n, :], scale=1.0 / D).then_inc(s_sd, 1)

            def in_high(i, t):
                act.wait_ge(s_xT, i + 1)
                A(in_cols(in_hi, t), in_psum(t), ACT.Copy).then_inc(s_inhi, 1)

            for i, t in enumerate(ORDER):
                token_root(i, t)
                if 2 <= i <= 3:
                    in_high(i - 2, ORDER[i - 2])
                if i == 3:
                    high(0)
                    in_high(2, ORDER[2])
            for i in (3, 4):
                in_high(i, ORDER[i])
            high(1)
            act.wait_ge(s_const, 8)
            A(ident_r[:, :], ident[:, :], ACT.Copy).then_inc(s_constr, 1)
            A(mask_r[:, :], mask[:, :], ACT.Copy).then_inc(s_constr, 1)
            act.wait_ge(s_pT, 1)
            A(prm[:, :], pTO[:, 512:512 + KT * NR], ACT.Copy).then_inc(s_sig, 1)
            act.wait_ge(s_sig, 1)
            high(2)
            act.wait_ge(s_f, 2)
            A(f_e, f_e, ACT.Abs).then_inc(s_f, 1)
            act.wait_ge(s_f, 3)
            A(f_e, f_e, ACT.Exp, scale=-1.0).then_inc(s_f, 1)
            act.wait_ge(s_f, 4)
            A(f_e, f_e, ACT.Ln, bias=ones[0:H, 0:1]).then_inc(s_f, 1)

            with act.Fori(0, KT // 2) as it:
                for j in range(2):
                    m = it * 2 + j
                    act.wait_ge(s_mm, it * 4 + (N_GLU + 2 * j + 1))
                    act.wait_ge(s_u, it * 2 + (j + 1))
                    A(vT[:, :], prod(N_GLU + 2 * j, T), ACT.Sigmoid, bias=par(R_BGS, m)).then_inc(s_sig, 1)
                    high(N_GLU + 2 * j + 2, it)
                    high(N_GLU + 2 * j + 3, it)
            act.wait_ge(s_f, 7)
            A(dec_rows[:, 0, :], f_m, ACT.Copy).then_inc(s_f, 1)

            def softmax(s, k, it=None):
                U = 8 * k + s
                wait(act, s_max, U + 1, it, 16)
                wait(act, s_T, U - 1, it, 16)
                nk = META + P * (s % QT + 1)
                A(prob[:, s % 2, 0:nk], scores(s % QT), ACT.Exp, bias=nmax[:, s:s + 1],
                  accum_out=rsum[:, s:s + 1]).then_inc(s_exp, 1)

            def probs_real(s, k, it=None):
                U = 8 * k + s
                wait(act, s_T, U + 1, it, 16)
                wait(act, s_pv, U - 1, it, 16)
                nr = P * (s % QT + 1)
                A(pT_meta[:, s % 2, :], pO7[0:META, 0:P], ACT.Copy).then_inc(s_pm, 1)
                A(pT[:, s % 2, 0:nr], pT6[:, 0:nr], ACT.Copy).then_inc(s_pr, 1)

            def out_high(k, it=None):
                wait(act, s_oT, k + 1, it, 2)
                A(feat(mid_hi, count(k, it, 2)), pT6, ACT.Copy).then_inc(s_ohi, 1)

            def pair_step(s, k, it=None):
                c = N_PAIR + 4 * k + s // 2
                if s % 2 == 0 and c > N_PAIR:
                    wait(act, s_mm, c, it, 8)
                if s == 0 and k > 0:
                    A(feat(ga, count(k - 1, it, 2)), prod(c - 1), ACT.Copy).then_inc(s_gev, 1)
                if s == 2:
                    if k == 0:
                        act.wait_ge(s_u, KT + 1)
                    wait(act, s_vT, 2 * k, it, 4)
                    A(vT[:, :], prod(c - 1, T), ACT.Copy).then_inc(s_vev, 1)
                if s in (4, 6):
                    dst, width, scale, done = (q_a, NT, HD ** -0.5, s_qh) if s == 4 else (k_a, T, 1.0, s_kh)
                    for h in range(2):
                        A(dst[0:HD, k % 2, h, :], prod(c - 1, width)[h * HD:(h + 1) * HD, :], ACT.Copy,
                          scale=scale).then_inc(done, 1)
                attention_step(s, k, it)
                if s == 4:
                    wait(act, s_qh, 2 * k + 2, it, 4)
                    A(q_b[0:HD, k % 2, :, :], q_a[0:HD, k % 2, :, :].bitcast(F32), ACT.Copy).then_inc(s_dup, 1)
                if s == 6:
                    wait(act, s_kh, 2 * k + 2, it, 4)
                    A(k_a[HD:P, k % 2, :, :], k_a[0:HD, k % 2, :, :].bitcast(F32), ACT.Copy).then_inc(s_dup, 1)
                if s % 2 == 0 and c > N_PAIR:
                    high(c + 1, it, 8)
                if s == 4:
                    wait(act, s_vT, 2 * k + 1, it, 4)
                    A(v_real[:, k % 2, :], pT6, ACT.Copy).then_inc(s_v, 1)
                if s == 5:
                    wait(act, s_vT, 2 * k + 2, it, 4)
                    A(v_meta[:, k % 2, :], pT6[0:META, 0:P], ACT.Copy).then_inc(s_v, 1)

            def attention_step(s, k, it=None):
                if s == 0 and k >= 2:
                    probs_real(7, k - 2, it)
                if s > 0 and 1 <= k <= PAIRS:
                    probs_real(s - 1, k - 1, it)
                if 1 <= k <= PAIRS:
                    softmax(s, k - 1, it)
                if s == 2 and k >= 2:
                    out_high(k - 2, it)

            for k in range(2):
                for s in range(8):
                    pair_step(s, k)
            with act.Fori(0, PAIRS // 2 - 1) as it:
                for k in (2, 3):
                    for s in range(8):
                        pair_step(s, k, it)
            for k in (PAIRS, PAIRS + 1):
                for s in range(8):
                    c = N_PAIR + 4 * k + s // 2
                    if s % 2 == 0:
                        act.wait_ge(s_mm, c)
                        if c == N_GC:
                            A(feat(ga, KT - 1), prod(c - 1), ACT.Copy).then_inc(s_gev, 1)
                        else:
                            m = c - 1 - N_GC
                            act.wait_ge(s_conv, KT * (TAPS_EARLY + TAPS_MID) + TAPS_LATE * (m + 1))
                            A(conv_gate(m), prod(c - 1), ACT.Copy).then_inc(
                                s_gev if c < N_AO - 1 else s_ev, 1)
                    if s % 2 == 0 and k > PAIRS:
                        high(c + 1)
                    attention_step(s, k)
                    if s % 2 == 0 and k == PAIRS:
                        high(c + 1)
                    if k > PAIRS and s == 2:
                        act.wait_ge(s_mu, 1)
                        A(bc[:, 0, :], pS[:, 0:NT], ACT.Copy).then_inc(s_mus, 1)
                    if k > PAIRS and 3 <= s <= 6:
                        for m in (2 * s - 6, 2 * s - 5):
                            act.wait_ge(s_xc, m + 1)
                            wait(act, s_sqsum, m)
                            A(prob[:, m % 2, 0:NT], feat(cv, m), ACT.Square).then_inc(s_sq, 1)
            act.wait_ge(s_var, 1)
            A(bc[:, 1, :], pS[:, NT:2 * NT], ACT.Sqrt, bias=eps_ln[:, :]).then_inc(s_lsd, 1)
            act.wait_ge(s_mm, N_AO)
            A(conv_gate(KT - 1), prod(N_AO - 1), ACT.Copy).then_inc(s_ev, 1)
            act.wait_ge(s_ev, 2)

            def conv_high(m):
                act.wait_ge(s_s, m + 1)
                A(feat_in(in_hi, m), feat(cv, m), ACT.Copy).then_inc(s_chi, 1)

            for m in range(KT):
                if m != 1:
                    high(N_AO + m + 1)
                A(feat(ga, m), feat(ga, m), ACT.Sigmoid).then_inc(s_gas, 1)
                if m == 0:
                    high(N_AO + 2)
                act.wait_ge(s_t, m + 1)
                A(pT[:, m % 2, :], feat(cv, m), ACT.Identity, bias=par(R_LB, m), scale=par(R_LG, m)).then_inc(s_y, 1)
                A(prob[:, m % 2, 0:NT], feat(cv, m), ACT.Sigmoid, bias=par(R_LB, m), scale=par(R_LG, m)).then_inc(s_y, 1)
                A(conv_gate(m), conv_gate(m), ACT.Sigmoid).then_inc(s_gcs, 1)
                if m:
                    conv_high(m - 1)
            conv_high(KT - 1)
            with act.Fori(0, KT // 4) as it:
                for j in range(4):
                    m = it * 4 + j
                    high(N_CO + j + 1, it)
                    act.wait_ge(s_mix, m + 1)
                    A(feat(mid_hi, m), feat(ga, m), ACT.Copy).then_inc(s_mhi, 1)
            for m in range(KT):
                high(N_WO + m + 1)
                act.wait_ge(s_rT, m + 1)
                A(feat(res, m), pT6 if m % 2 == 0 else pO7, ACT.Copy).then_inc(s_res, 1)
                act.wait_ge(s_ev, N_WO + m - N_AO + 3)
                wait(act, s_hacc, m)
                A(prob[:, m % 2, 0:NT], feat(res, m), ACT.Square).then_inc(s_hsq, 1)
                A(feat_in(in_hi, m), feat(res, m), ACT.Copy, scale=par(R_G2, m)).then_inc(s_ghi, 1)

            def mlp(k, it=None, last=False):
                for j in range(KT):
                    c = N_MLP + 2 * KT * k + j
                    if not (k == 0 and j == 1):
                        high(c + 1, it, 2 * KT)
                    if k == 0 and j == 0:
                        act.wait_ge(s_hsum, 1)
                        A(bc[:, 0, :], pS[:, 0:NT], ACT.Sqrt, bias=eps_rms[:, :]).then_inc(s_hsd, 1)
                        high(c + 2)
                    wait(act, s_relu, KT * k + j + 1, it, KT)
                    A(prob[:, j % 2, 0:NT], pT[:, j % 2, :], ACT.Square).then_inc(s_hf, 1)
                    wait(act, s_hf, KT * k + j + 1, it, KT)
                    A(feat(mid_hi, j), prob[:, j % 2, 0:NT], ACT.Copy).then_inc(s_fhi, 1)
                for j in range(KT):
                    c = N_MLP + 2 * KT * k + KT + j
                    if c + 1 < N_ALL:
                        high(c + 1, it, 2 * KT)

            mlp(0)
            with act.Fori(0, BLOCKS - 2) as it:
                mlp(1, it)
            mlp(BLOCKS - 1)
            for t in range(QT):
                act.wait_ge(s_yT, t + 1)
                wait(act, s_yss, t)
                A(junk[:, 0:D], y_psum(t), ACT.Square, accum_out=ss[:, t:t + 1]).then_inc(s_yss, 1)
                act.wait_ge(s_yss, t + 1)
                A(sd[:, t:t + 1], ss[:, t:t + 1], ACT.Sqrt, bias=eps_rms[:, :], scale=1.0 / D).then_inc(s_ysd, 1)

        @block.vector
        def _(dve):
            V = nc.vector

            def low(c, it=None, per=4):
                wait(dve, s_hi, c + 1, it, per)
                V.tensor_tensor(w_lo[:, c % SPLIT, :], raw[:, c % RAW, :], w_hi[:, c % SPLIT, :].bitcast(F32),
                                ALU.subtract).then_inc(s_lo, 1)

            V.memset(f_one, 1.0).then_inc(s_one, 1)
            V.memset(q_b[HD:HD + 2, :, :, :].bitcast(F32), 1.0).then_inc(s_one2, 1)
            dve.wait_ge(s_g1, 16)

            def scale_tokens(i, t):
                n = P if t < QT else META
                dve.wait_ge(s_sd, i + 2)
                V.reciprocal(rstd[0:n, t:t + 1], sd[0:n, t:t + 1]).then_inc(s_rstd, 1)
                dve.wait_ge(s_rstd, i + 1)
                V.scalar_tensor_tensor(out=xs_tok[:, t, :] if t < QT else xs_meta,
                                       in0=x_tok[:, t, :] if t < QT else x_meta, scalar=rstd[0:n, t:t + 1],
                                       in1=gain_in[0:n, :], op0=ALU.mult, op1=ALU.mult).then_inc(s_xs, 1)

            def in_low(i, t):
                dve.wait_ge(s_inhi, i + 1)
                V.tensor_tensor(in_cols(in_lo, t), in_psum(t), in_cols(in_hi, t).bitcast(F32),
                                ALU.subtract).then_inc(s_inlo, 1)

            for i, t in enumerate(ORDER):
                scale_tokens(i, t)
                if 2 <= i <= 3:
                    in_low(i - 2, ORDER[i - 2])
                if i == 3:
                    low(0)
                    in_low(2, ORDER[2])
            for i in (3, 4):
                in_low(i, ORDER[i])
            low(1)
            dve.wait_ge(s_sig, 1)
            dve.wait_ge(s_xs, QT + 1)
            V.memset(u[:, :].rearrange("p (m t) -> p m t", t=UW)[:, :, 0:PAD], 0.0).then_inc(s_u, 1)
            dve.wait_ge(s_mm, N_F + 1)
            dve.wait_ge(s_bf, 16)
            V.tensor_scalar(f_e, prod(N_F, T)[0:H, :], bf[:, :], None, ALU.add).then_inc(s_f, 1)
            V.tensor_scalar(f_m, prod(N_F, T)[0:H, :], bf[:, :], 0.0, ALU.add, ALU.min).then_inc(s_f, 1)
            low(2)
            dve.wait_ge(s_f, 5)
            V.tensor_tensor(f_l, f_e, f_m, ALU.subtract).then_inc(s_f, 1)
            dve.wait_ge(s_f, 6)
            dve.wait_ge(s_one, 1)
            V.tensor_tensor_scan(f_m, f_one, f_l, 0.0, ALU.mult, ALU.add).then_inc(s_f, 1)

            def tap(j, m, done):
                dst = feat(cv, m)
                src = u[:, ds(m * UW + j, NT)]
                if j == 0:
                    V.tensor_scalar(dst, src, par(0, m), par(R_CB, m), ALU.mult, ALU.add).then_inc(s_conv, 1)
                else:
                    dve.wait_ge(s_conv, done)
                    V.scalar_tensor_tensor(out=dst, in0=src, scalar=par(j, m), in1=dst, op0=ALU.mult,
                                           op1=ALU.add).then_inc(s_conv, 1)

            with dve.Fori(0, KT // 2) as it:
                for jj in range(2):
                    m = it * 2 + jj
                    g = N_GLU + 2 * jj
                    low(g + 2, it)
                    dve.wait_ge(s_mm, it * 4 + (g + 2))
                    dve.wait_ge(s_sig, it * 2 + (jj + 2))
                    V.scalar_tensor_tensor(out=u[:, ds(m * UW + PAD, T)], in0=prod(g + 1, T), scalar=par(R_BGV, m),
                                           in1=vT[:, :], op0=ALU.add, op1=ALU.mult).then_inc(s_u, 1)
                    dve.wait_ge(s_u, it * 2 + (jj + 2))
                    for j in range(TAPS_EARLY):
                        if j == 3:
                            low(g + 3, it)
                        tap(j, m, it * (2 * TAPS_EARLY) + (jj * TAPS_EARLY + j))

            dve.wait_ge(s_f, 8)
            V.tensor_tensor(dec_rows[:, 1, :], f_m, dec_rows[:, 0, :].bitcast(F32), ALU.subtract).then_inc(s_f, 1)

            def row_max(s, k, it=None):
                U = 8 * k + s
                wait(dve, s_S, U + 1, it, 16)
                V.tensor_reduce(nmax[:, s:s + 1], scores(s % QT), AX_X, ALU.max, negate=True).then_inc(s_max, 1)

            def sum_reciprocal(s, k, it=None):
                U = 8 * k + s
                wait(dve, s_exp, U + 1, it, 16)
                V.reciprocal(rinv[:, s:s + 1], rsum[:, s:s + 1]).then_inc(s_rinv, 1)

            def head_out(s, k, it=None):
                U = 8 * k + s
                wait(dve, s_pv, U + 1, it, 16)
                wait(dve, s_rinv, U + 1, it, 16)
                at = (s % QT) * P + (s // QT) * HD
                V.tensor_scalar(o_sb[:, k % 2, at:at + HD], pO7[:, P:P + HD], rinv[:, s:s + 1], None,
                                ALU.mult).then_inc(s_o, 1)

            def taps(s, k, it, first, last):
                for i in range(sum(TAPS_STEP[:s]) + first, sum(TAPS_STEP[:s]) + last):
                    tap(TAPS_EARLY + TAPS_MID + i, count(k - 1, it, 2),
                        count(KT * (TAPS_EARLY + TAPS_MID) + TAPS_LATE * (k - 1) + i, it, 2 * TAPS_LATE))

            def attention_step(s, k, it=None):
                if 1 <= k <= PAIRS:
                    row_max(s, k - 1, it)
                if s in (4, 6) and k < PAIRS:
                    c = N_PAIR + 4 * k + s // 2 - 1
                    hi, dst, rows, width, scale, ready, done = (
                        (q_a, q_a, slice(HD, P), NT, HD ** -0.5, s_qh, s_ql) if s == 4 else
                        (k_a, k_b, slice(0, HD), T, 1.0, s_kh, s_kl))
                    for h in range(2):
                        wait(dve, ready, 2 * k + 2, it, 4)
                        V.scalar_tensor_tensor(out=dst[rows, k % 2, h, :], in0=prod(c, width)[h * HD:(h + 1) * HD, :],
                                               scalar=scale, in1=hi[0:HD, k % 2, h, :].bitcast(F32), op0=ALU.mult,
                                               op1=ALU.subtract).then_inc(done, 1)
                if s % 2 == 0 and k == 0 and s > 0:
                    low(N_PAIR + s // 2 + 1)
                if k == 0:
                    for i in range(sum(MID_STEP[:s]), sum(MID_STEP[:s + 1])):
                        j, m = divmod(i, KT)
                        tap(TAPS_EARLY + j, m, KT * (TAPS_EARLY + j) if j == 0 else KT * TAPS_EARLY + i - KT + 1)
                elif k <= PAIRS:
                    taps(s, k, it, 0, 1)
                before = (7, k - 2) if s == 0 else (s - 1, k - 1)
                has = k >= 2 if s == 0 else 1 <= k <= PAIRS
                if has:
                    sum_reciprocal(*before, it)
                if 1 <= k <= PAIRS:
                    taps(s, k, it, 1, TAPS_STEP[s])
                if has:
                    head_out(*before, it)
                if s == 2 and k >= 2:
                    wait(dve, s_ohi, k - 1, it, 2)
                    V.tensor_tensor(feat(mid_lo, count(k - 2, it, 2)), pT6,
                                    feat(mid_hi, count(k - 2, it, 2)).bitcast(F32), ALU.subtract).then_inc(s_olo, 1)

            def pair_step(s, k, it=None):
                c = N_PAIR + 4 * k + s // 2
                attention_step(s, k, it)
                if s % 2 == 0 and k > 0:
                    low(c + 1, it, 8)

            for k in range(2):
                for s in range(8):
                    pair_step(s, k)
            with dve.Fori(0, PAIRS // 2 - 1) as it:
                for k in (2, 3):
                    for s in range(8):
                        pair_step(s, k, it)
            for k in (PAIRS, PAIRS + 1):
                for s in range(8):
                    if k <= PAIRS:
                        pair_step(s, k)
                        continue
                    if s % 2 == 0:
                        low(N_PAIR + 4 * k + s // 2 + 1)
                    attention_step(s, k)
                    if s == 2:
                        dve.wait_ge(s_mus, 1)
                    for m in {2: range(5), 4: range(5, KT)}.get(s, ()):
                        V.tensor_tensor(feat(cv, m), feat(cv, m), bc[:, 0, :], ALU.subtract).then_inc(s_xc, 1)
                    for m in {5: (SQ_POOL,), 6: range(SQ_POOL + 1, KT)}.get(s, ()):
                        dve.wait_ge(s_sq, m + 1)
                        dve.wait_ge(s_sqsum, m + 1)
                        V.tensor_tensor(sq_sum, sq_sum, prob[:, m % 2, 0:NT], ALU.add).then_inc(s_sqsum, 1)
            low(N_AO + 1)
            dve.wait_ge(s_lsd, 1)
            V.reciprocal(bc[:, 1, :], bc[:, 1, :]).then_inc(s_lr, 1)
            dve.wait_ge(s_lr, 1)

            def silu(m):
                dve.wait_ge(s_y, 2 * m + 2)
                V.tensor_tensor(feat(cv, m), pT[:, m % 2, :], prob[:, m % 2, 0:NT], ALU.mult).then_inc(s_s, 1)
                dve.wait_ge(s_chi, m + 1)
                V.tensor_tensor(feat_in(in_lo, m), feat(cv, m), feat_in(in_hi, m).bitcast(F32),
                                ALU.subtract).then_inc(s_clo, 1)

            for m in range(KT):
                c = N_AO + m
                V.tensor_tensor(feat(cv, m), feat(cv, m), bc[:, 1, :], ALU.mult).then_inc(s_t, 1)
                if m:
                    low(c + 1)
                if m:
                    silu(m - 1)
                dve.wait_ge(s_mm, c + 1)
                dve.wait_ge(s_gas, m + 1)
                V.tensor_tensor(feat(ga, m), prod(c), feat(ga, m), ALU.mult).then_inc(s_ev, 1)
            silu(KT - 1)
            with dve.Fori(0, KT // 4) as it:
                for j in range(4):
                    m = it * 4 + j
                    c = N_CO + j
                    low(c + 1, it)
                    dve.wait_ge(s_mm, it * 4 + (c + 1))
                    dve.wait_ge(s_gcs, m + 1)
                    V.scalar_tensor_tensor(out=pT[:, j % 2, :], in0=prod(c), scalar=par(R_CO, m), in1=conv_gate(m),
                                           op0=ALU.add, op1=ALU.mult).then_inc(s_ev, 1)
                    dve.wait_ge(s_ev, it * 4 + (c - N_AO + 3))
                    V.tensor_tensor(feat(ga, m), pT[:, j % 2, :], feat(ga, m), ALU.add).then_inc(s_mix, 1)
                    dve.wait_ge(s_mhi, m + 1)
                    V.tensor_tensor(feat(mid_lo, m), feat(ga, m), feat(mid_hi, m).bitcast(F32),
                                    ALU.subtract).then_inc(s_mlo, 1)
            V.memset(bc[:, 1, :], 0.0).then_inc(s_hacc, 1)
            for m in range(KT):
                c = N_WO + m
                low(c + 1)
                dve.wait_ge(s_mm, c + 1)
                dve.wait_ge(s_res, m + 1)
                V.tensor_tensor(feat(res, m), prod(c), feat(res, m), ALU.add).then_inc(s_ev, 1)
                dve.wait_ge(s_hsq, m + 1)
                dve.wait_ge(s_hacc, m + 1)
                V.tensor_tensor(bc[:, 1, :], bc[:, 1, :], prob[:, m % 2, 0:NT], ALU.add).then_inc(s_hacc, 1)
                dve.wait_ge(s_ghi, m + 1)
                V.scalar_tensor_tensor(out=feat_in(in_lo, m), in0=feat(res, m), scalar=par(R_G2, m),
                                       in1=feat_in(in_hi, m).bitcast(F32), op0=ALU.mult,
                                       op1=ALU.subtract).then_inc(s_glo, 1)

            def mlp(k, it=None, last=False):
                for j in range(KT):
                    c = N_MLP + 2 * KT * k + j
                    if not (k == 0 and j == 1):
                        low(c + 1, it, 2 * KT)
                    if k == 0 and j == 0:
                        dve.wait_ge(s_hsd, 1)
                        V.reciprocal(bc[:, 0, :], bc[:, 0, :]).then_inc(s_hr, 1)
                        low(c + 2)
                        dve.wait_ge(s_hr, 1)
                    wait(dve, s_mm, c + 1, it, 2 * KT)
                    V.scalar_tensor_tensor(out=pT[:, j % 2, :], in0=prod(c), scalar=0.0, in1=bc[:, 0, :],
                                           op0=ALU.max, op1=ALU.mult).then_inc(s_relu, 1)
                    wait(dve, s_fhi, KT * k + j + 1, it, KT)
                    V.tensor_tensor(feat(mid_lo, j), prob[:, j % 2, 0:NT], feat(mid_hi, j).bitcast(F32),
                                    ALU.subtract).then_inc(s_flo, 1)
                for j in range(KT):
                    c = N_MLP + 2 * KT * k + KT + j
                    if c + 1 < N_ALL:
                        low(c + 1, it, 2 * KT)
                    if last and j >= KT - 2:
                        continue
                    wait(dve, s_mm, c + 1, it, 2 * KT)
                    V.tensor_tensor(feat(res, j), prod(c), feat(res, j), ALU.add).then_inc(s_acc, 1)

            mlp(0)
            with dve.Fori(0, BLOCKS - 2) as it:
                mlp(1, it)
            mlp(BLOCKS - 1, last=True)

            def add_half(i):
                c, h = HALVES[i]
                dve.wait_ge(s_half, i + 1)
                at = (c - N_ALL + KT) * NT + h * HT
                V.tensor_tensor(res[:, at:at + HT], half_prod(c, h), res[:, at:at + HT], ALU.add).then_inc(s_acc, 1)

            for i in range(3):
                add_half(i)
            dve.wait_ge(s_gain, 16)
            for t in range(QT):
                if t == 2:
                    add_half(3)
                dve.wait_ge(s_ysd, t + 1)
                V.reciprocal(rstd[:, t:t + 1], sd[:, t:t + 1]).then_inc(s_yr, 1)
                dve.wait_ge(s_yr, t + 1)
                V.scalar_tensor_tensor(out=y_tok[:, t, :], in0=y_psum(t), scalar=rstd[:, t:t + 1], in1=gain_bc,
                                       op0=ALU.mult, op1=ALU.mult).then_inc(s_y4, 1)

        @block.tensor
        def _(pe):
            mm = nc.tensor.matmul

            total = 3 * KT

            def chunk(c, i0, i1, rhs_hi, rhs_lo, width=NT, first=None):
                stride = T if rhs_hi is in_hi else NT
                full = width == T
                base = META if c < N_AO and not full else 0
                for i in range(i0, i1):
                    kt, what = divmod(i, 3)
                    if first is not None and what == 0:
                        first(kt)
                    wt = (w_hi, w_hi, w_lo)[what][:, c % SPLIT, kt * P:(kt + 1) * P]
                    src = (rhs_hi, rhs_lo, rhs_hi)[what]
                    flags = dict(start=i == 0, stop=i == total - 1)
                    if full:
                        for h in range(2):
                            last = mm(prod(c, T)[:, h * HALF:(h + 1) * HALF], wt,
                                      src[:, kt * T + h * HALF:kt * T + (h + 1) * HALF], **flags)
                    else:
                        at = kt * stride + base
                        last = mm(prod(c), wt, src[:, at:at + NT], **flags)
                if i1 == total:
                    last.then_inc(s_mm, 1)

            def begin(c, it=None, per=4):
                wait(pe, s_lo, c + 1, it, per)
                wait(pe, s_ev, c - N_AO + 1, it, per)

            def tokens_transpose(i, t):
                pe.wait_ge(s_xs, i + 1)
                if i >= 3:
                    pe.wait_ge(s_inlo, i - 2)
                for m in range(KT):
                    src = xs_tok[:, t, m * P:(m + 1) * P] if t < QT else xs_meta[:, m * P:(m + 1) * P]
                    n = P if t < QT else META
                    last = nc.tensor.transpose(in_psum(t)[:, m, :], src, ident[0:n, 0:n])
                last.then_inc(s_xT, 1)

            def forget_products(h, kt0, kt1):
                for i in range(3 * kt0, 3 * kt1):
                    kt, what = divmod(i, 3)
                    last = mm(prod(N_F, T)[:, h * HALF:(h + 1) * HALF],
                              (w_hi, w_hi, w_lo)[what][:, N_F % SPLIT, kt * P:(kt + 1) * P],
                              (in_hi, in_lo, in_hi)[what][:, kt * T + h * HALF:kt * T + (h + 1) * HALF],
                              start=i == 0, stop=i == 3 * KT - 1)
                return last

            pe.wait_ge(s_const, 8)
            for i in range(QT):
                tokens_transpose(i, ORDER[i])
            pe.wait_ge(s_lo, 1)
            pe.wait_ge(s_inlo, 3)
            forget_products(0, 0, KT // 2)
            tokens_transpose(QT, ORDER[QT])
            forget_products(0, KT // 2, KT)
            pe.wait_ge(s_par, 16 * 7)
            for m in range(KT):
                last = nc.tensor.transpose(pTO[:, 512 + m * NR:512 + (m + 1) * NR], prow[:, m * P:(m + 1) * P],
                                           ident[0:NR, 0:NR])
            last.then_inc(s_pT, 1)
            pe.wait_ge(s_inlo, QT + 1)
            forget_products(1, 0, KT).then_inc(s_mm, 1)

            with pe.Fori(0, KT // 2) as it:
                for j in range(2):
                    g = N_GLU + 2 * j
                    pe.wait_ge(s_lo, it * 4 + (g + 1))
                    pe.wait_ge(s_sig, it * 2 + (j + 1))
                    chunk(g, 0, total, in_hi, in_lo, T)
                    pe.wait_ge(s_lo, it * 4 + (g + 2))
                    pe.wait_ge(s_u, it * 2 + (j + 1))
                    pe.wait_ge(s_f, 2)
                    chunk(g + 1, 0, total, in_hi, in_lo, T)

            def unit_scores(s, k, it=None):
                U = 8 * k + s
                h, q = divmod(s, QT)
                if s == 0:
                    wait(pe, s_dup, 2 * k + 2, it, 4)
                    wait(pe, s_ql, 2 * k + 2, it, 4)
                    wait(pe, s_kl, 2 * k + 2, it, 4)
                    wait(pe, s_dec[k % 2], 16 * (k // 2 + 1), it, 16)
                wait(pe, s_exp, U if q in (0, 3) else U - 1, it, 16)
                dst = scores(q)
                nk = META + P * (q + 1)
                rows = HD + 2
                for a, b in (((0, nk),) if q < 3 else ((0, HALF), (HALF, nk))):
                    diagonal = b == nk
                    mm(dst[:, a:b], q_a[:, k % 2, h, q * P:(q + 1) * P], k_a[:, k % 2, h, a:b], start=True, stop=False)
                    last = mm(dst[:, a:b], q_b[0:rows, k % 2, h, q * P:(q + 1) * P], k_b[0:rows, k % 2, h, a:b],
                              start=False, stop=not diagonal)
                    if diagonal:
                        last = mm(dst[:, nk - P:nk], ident_r[:, :], mask_r[:, :], start=False, stop=True)
                last.then_inc(s_S, 1)

            def unit_transpose(s, k, it=None):
                U = 8 * k + s
                wait(pe, s_exp, U + 1, it, 16)
                wait(pe, s_o, U, it, 16)
                wait(pe, s_pr, U, it, 16)
                nc.tensor.transpose(pO7[:, 0:P], prob[:, s % 2, 0:P], ident[:, :])
                for t in range(s % QT + 1):
                    last = nc.tensor.transpose(pT6[:, t * P:(t + 1) * P],
                                               prob[:, s % 2, META + t * P:META + (t + 1) * P], ident[:, :])
                last.then_inc(s_T, 1)

            def unit_out(s, k, it=None):
                U = 8 * k + s
                h, q = divmod(s, QT)
                wait(pe, s_pr, U + 1, it, 16)
                wait(pe, s_pm, U + 1, it, 16)
                if s == 0:
                    wait(pe, s_v, 2 * k + 2, it, 4)
                dst = pO7[:, P:P + HD]
                mm(dst, pT_meta[:, s % 2, :], v_meta[:, k % 2, h * HD:(h + 1) * HD], start=True, stop=False)
                for t in range(q + 1):
                    last = mm(dst, pT[:, s % 2, t * P:(t + 1) * P],
                              v_real[:, k % 2, t * P + h * HD:t * P + (h + 1) * HD], start=False, stop=t == q)
                last.then_inc(s_pv, 1)

            CUTS = (0, 4, 7, total // 2)

            def pair_step(s, k, it=None):
                c = N_PAIR + 4 * k + s // 2
                width = T if k < PAIRS and s // 2 in (0, 2) else NT
                at = [total // 2 * (s % 2) + i for i in CUTS]
                if s % 2 == 0:
                    wait(pe, s_lo, c + 1, it, 8)
                    if k < PAIRS:
                        signal, n, per = ((s_kl, 2 * k, 4), (s_gev, k, 2), (s_vev, k + 1, 2), (s_ql, 2 * k + 2, 4))[s // 2]
                    elif c == N_GC:
                        signal, n, per = s_kl, 2 * PAIRS, 0
                    else:
                        signal, n, per = s_gev, c - N_GC + PAIRS - 1, 0
                    wait(pe, signal, n, it, per)
                if k == 0 and s == 2:
                    pe.wait_ge(s_u, KT + 1)
                chunk(c, at[0], at[1], in_hi, in_lo, width)
                has = k >= 2 if s == 0 else 1 <= k <= PAIRS
                before = (7, k - 2) if s == 0 else (s - 1, k - 1)
                if 1 <= k <= PAIRS:
                    unit_scores(s, k - 1, it)
                chunk(c, at[1], at[2], in_hi, in_lo, width)
                if has:
                    if s == 3 and k >= 2:
                        wait(pe, s_olo, k - 1, it, 2)
                    if k < PAIRS and s in (5, 6):
                        wait(pe, s_v, 2 * k + s - 4, it, 4)
                    unit_transpose(*before, it)
                chunk(c, at[2], at[3], in_hi, in_lo, width)
                if has:
                    unit_out(*before, it)
                if s == 2 and k >= 2:
                    pair_out(k - 2, it)
                if k < PAIRS and s == 4:
                    wait(pe, s_vev, k + 1, it, 2)
                    for t in range(QT):
                        last = nc.tensor.transpose(pT6[:, t * P:(t + 1) * P], vT[:, META + t * P:META + (t + 1) * P],
                                                   ident[:, :])
                    last.then_inc(s_vT, 1)
                if k < PAIRS and s == 5:
                    wait(pe, s_v, 2 * k + 1, it, 4)
                    nc.tensor.transpose(pT6[:, 0:P], vT[:, 0:P], ident[:, :]).then_inc(s_vT, 1)

            def pair_out(k, it=None):
                wait(pe, s_o, 8 * k + 8, it, 16)
                for q in range(QT):
                    last = nc.tensor.transpose(pT6[:, q * P:(q + 1) * P], o_sb[:, k % 2, q * P:(q + 1) * P], ident[:, :])
                last.then_inc(s_oT, 1)

            pe.wait_ge(s_sig, KT + 1)
            pe.wait_ge(s_constr, 2)
            pe.wait_ge(s_one2, 1)
            for k in range(2):
                for s in range(8):
                    pair_step(s, k)
            with pe.Fori(0, PAIRS // 2 - 1) as it:
                for k in (2, 3):
                    for s in range(8):
                        pair_step(s, k, it)
            for s in range(8):
                pair_step(s, PAIRS)
            for s in range(8):
                pair_step(s, PAIRS + 1)
                if s == 1:
                    pe.wait_ge(s_csum, KT + 1)
                    pe.wait_ge(s_exp, 8 * PAIRS)
                    mm(pS[:, 0:NT], mean_w[:, :], conv_sum[:, :], start=True, stop=True).then_inc(s_mu, 1)
                if s == 7:
                    pe.wait_ge(s_sqsum, KT + 1)
                    mm(pS[:, NT:2 * NT], mean_w[:, :], sq_sum, start=True, stop=True).then_inc(s_var, 1)

            for n0, hi, lo, ready in ((N_AO, mid_hi, mid_lo, s_olo), (N_CO, in_hi, in_lo, s_clo)):
                with pe.Fori(0, KT // 4) as it:
                    for j in range(4):
                        begin(n0 + j, it)
                        chunk(n0 + j, 0, total, hi, lo,
                              first=(lambda kt: pe.wait_ge(ready, kt + 1)) if j == 0 else None)

            for m in range(KT):
                c = N_WO + m
                begin(c)
                wait(pe, s_again, 16 if m == 0 else 0)
                for t in range(QT):
                    last = nc.tensor.transpose((pT6 if m % 2 == 0 else pO7)[:, t * P:(t + 1) * P],
                                               x_again[:, t, m * P:(m + 1) * P], ident[:, :])
                last.then_inc(s_rT, 1)
                chunk(c, 0, total, mid_hi, mid_lo, first=(lambda kt: pe.wait_ge(s_mlo, kt + 1)) if m == 0 else None)

            def mlp_begin(c, k, j, it, up):
                wait(pe, s_lo, c + 1, it, 2 * KT)
                if k == 0 and up and j < 2:
                    pe.wait_ge(s_ev, c - N_AO + 1)
                elif up and j < 2:
                    wait(pe, s_acc, KT * k - 1 + j, it, KT)
                elif up:
                    wait(pe, s_relu, KT * k + j - 1, it, KT)
                elif j < 2:
                    wait(pe, s_relu, KT * (k + 1) - 1 + j, it, KT)
                else:
                    wait(pe, s_acc, KT * k + j - 1, it, KT)

            def mlp(k, it=None, last=False):
                for j in range(KT):
                    c = N_MLP + 2 * KT * k + j
                    mlp_begin(c, k, j, it, True)
                    first = (lambda kt: pe.wait_ge(s_glo, kt + 1)) if k == 0 and j == 0 else None
                    chunk(c, 0, total // 2, in_hi, in_lo, first=first)
                    if k == 0 and j == 0:
                        pe.wait_ge(s_hacc, KT + 1)
                        mm(pS[:, 0:NT], mean_w[:, :], bc[:, 1, :], start=True, stop=True).then_inc(s_hsum, 1)
                    chunk(c, total // 2, total, in_hi, in_lo, first=first)
                for j in range(KT - 2 if last else KT):
                    c = N_MLP + 2 * KT * k + KT + j
                    mlp_begin(c, k, j, it, False)
                    chunk(c, 0, total, mid_hi, mid_lo,
                          first=(lambda kt: wait(pe, s_flo, KT * k + kt + 1, it, KT)) if j == 0 else None)

            mlp(0)
            with pe.Fori(0, BLOCKS - 2) as it:
                mlp(1, it)
            mlp(BLOCKS - 1, last=True)

            def half_chunk(i):
                c, h = HALVES[i]
                wait(pe, s_lo, c + 1)
                wait(pe, s_acc, KT * (BLOCKS - 1) + (c - 2) - (N_ALL - KT) + 1)
                for n in range(3 * KT):
                    kt, what = divmod(n, 3)
                    at = kt * NT + h * HT
                    last = mm(half_prod(c, h), (w_hi, w_hi, w_lo)[what][:, c % SPLIT, kt * P:(kt + 1) * P],
                              (mid_hi, mid_lo, mid_hi)[what][:, at:at + HT], start=n == 0, stop=n == 3 * KT - 1)
                last.then_inc(s_half, 1)

            def back(t):
                for m in range(KT):
                    need = KT * (BLOCKS - 1) + m + 1 + (2 if t >= 2 and m >= KT - 2 else 0)
                    pe.wait_ge(s_acc, max(need, KT * BLOCKS + (0, 0, 1, 2)[t] if t >= 2 else 0))
                    last = nc.tensor.transpose(y_psum(t)[:, m * P:(m + 1) * P], res[:, m * NT + t * P:m * NT + (t + 1) * P],
                                               ident[:, :])
                last.then_inc(s_yT, 1)

            half_chunk(0)
            half_chunk(1)
            half_chunk(2)
            back(0)
            back(1)
            half_chunk(3)
            back(2)
            back(3)


_INS = ["x", "meta_tokens", "norm_mix_gain", "w_in", "b_forget", "w_attn_out", "b_glu", "conv_dw_w", "conv_dw_b",
        "conv_ln_gain", "conv_ln_bias", "w_conv_out", "b_conv_out", "w_out", "norm_mlp_gain", "w_mlp_up",
        "w_mlp_down", "final_norm_gain"]
_OUTS = [((1, NT, D), "float32")]


def kernel(**inputs):
    import numpy as _np
    import concourse.bacc as _bacc
    from concourse import mybir as _mybir
    from concourse.bass_utils import run_bass_kernel_spmd as _run

    nc = _bacc.Bacc("TRN2", target_bir_lowering=False, num_devices=1)
    arrays, args = {}, []
    for name in _INS:
        a = _np.ascontiguousarray(inputs[name])
        arrays[f"in_{name}_dram"] = a
        args.append(nc.dram_tensor(f"in_{name}_dram", a.shape, _mybir.dt.from_np(a.dtype), kind="ExternalInput").ap())
    for i, (shape, dtype) in enumerate(_OUTS):
        dt = _mybir.dt.from_np(_np.dtype(dtype))
        args.append(nc.dram_tensor(f"out_{i}_dram", shape, dt, kind="ExternalOutput").ap())
    build(nc, *args)
    r = _run(nc, [arrays], core_ids=[0])
    got = tuple(r.results[0][f"out_{i}_dram"] for i in range(len(_OUTS)))
    return got[0]
```
